# Optimizing a Trainium2 kernel written in Bass

```python
import functools
import jax, jax.numpy as jnp
from jax import lax
import numpy as np

D_MODEL = 1024
BATCH = 1
SEQ = 1024
DEPTH = 1
DEC_BATCH = 8
DEC_SEQ = 8
PAST_LEN = 4096
PAGE_SIZE = 128

N_Q_HEADS = 8
N_KV_HEADS = 2
HEAD_DIM = 64
GQA_GROUP = N_Q_HEADS // N_KV_HEADS
WINDOW = 128
ATTN_BLOCK = WINDOW
ROPE_THETA = 10000.0
N_RET_HEADS = 4
RET_KEY_DIM = 128
RET_VAL_DIM = 256
RET_CHUNK = 128
RET_THETA = 10000.0
D_FF = ((8 * D_MODEL // 3 + 127) // 128) * 128
DEEPNORM_ALPHA = (2.0 * DEPTH) ** 0.25
DEEPNORM_BETA = (8.0 * DEPTH) ** -0.25
LN_EPS = 1e-5
GN_EPS = 1e-6
NEG_INF = -1e30
Q_W = N_Q_HEADS * HEAD_DIM
KV_W = N_KV_HEADS * HEAD_DIM
RQ_W = N_RET_HEADS * RET_KEY_DIM
RV_W = N_RET_HEADS * RET_VAL_DIM
IN_SPLITS = (Q_W, KV_W, KV_W, RQ_W, RQ_W, RV_W, RV_W, D_MODEL, D_MODEL)
VALUE_GROUPS = (2, 5)
N_IN = sum(IN_SPLITS)

kernel_name = 'hybrid_swa_sink_retention_macaron_deepnorm_step'

def layer_norm(x, g, b):
    xf = x.astype(jnp.float32)
    mu = jnp.mean(xf, axis=-1, keepdims=True)
    xc = xf - mu
    var = jnp.mean(xc * xc, axis=-1, keepdims=True)
    return (xc * lax.rsqrt(var + LN_EPS) * g.astype(jnp.float32) + b.astype(jnp.float32)).astype(x.dtype)

def group_norm(o):
    mu = jnp.mean(o, axis=-1, keepdims=True)
    oc = o - mu
    var = jnp.mean(oc * oc, axis=-1, keepdims=True)
    return oc * lax.rsqrt(var + GN_EPS)

def swiglu(x, wi, wo):
    g, u = jnp.split(x @ wi, 2, axis=-1)
    return (jax.nn.silu(g) * u) @ wo

def attn_inv_freq():
    return 1.0 / (ROPE_THETA ** (jnp.arange(0, HEAD_DIM, 2, dtype=jnp.float32) / HEAD_DIM))

def ret_inv_freq():
    return 1.0 / (RET_THETA ** jnp.linspace(0.0, 1.0, RET_KEY_DIM // 2, dtype=jnp.float32))

def rope(x, pos, inv_freq):
    ang = pos.astype(jnp.float32)[:, None] * inv_freq[None, :]
    c = jnp.cos(ang)[:, None, :]
    s = jnp.sin(ang)[:, None, :]
    xf = x.astype(jnp.float32)
    x1, x2 = jnp.split(xf, 2, axis=-1)
    return jnp.concatenate([x1 * c - x2 * s, x2 * c + x1 * s], axis=-1).astype(x.dtype)

def window_mask(qpos, kpos):
    return (kpos <= qpos) & (qpos - kpos < WINDOW) & (kpos >= 0)

def sink_softmax(s, mask, sinks):
    s = jnp.where(mask, s, NEG_INF)
    sink = jnp.broadcast_to(sinks.astype(jnp.float32).reshape(N_KV_HEADS, GQA_GROUP, 1, 1), s.shape[:-1] + (1,))
    p = jax.nn.softmax(jnp.concatenate([s, sink], axis=-1), axis=-1)
    return p[..., :-1]

def swa_prompt(q, k, v, sinks):
    B, S = q.shape[0], q.shape[1]
    L = ATTN_BLOCK
    nb = S // L
    qb = q.reshape(B, nb, L, N_KV_HEADS, GQA_GROUP, HEAD_DIM)
    kb = k.reshape(B, nb, L, N_KV_HEADS, HEAD_DIM)
    vb = v.reshape(B, nb, L, N_KV_HEADS, HEAD_DIM)
    pad = ((0, 0), (1, 0), (0, 0), (0, 0), (0, 0))
    k_band = jnp.concatenate([jnp.pad(kb[:, :-1], pad), kb], axis=2)
    v_band = jnp.concatenate([jnp.pad(vb[:, :-1], pad), vb], axis=2)
    s = jnp.einsum('bnqkgd,bnmkd->bnkgqm', qb, k_band).astype(jnp.float32) * (HEAD_DIM ** -0.5)
    blk = jnp.arange(nb, dtype=jnp.int32)[:, None] * L
    qpos = blk + jnp.arange(L, dtype=jnp.int32)[None, :]
    kpos = blk - L + jnp.arange(2 * L, dtype=jnp.int32)[None, :]
    mask = window_mask(qpos[:, :, None], kpos[:, None, :])[None, :, None, None]
    p = sink_softmax(s, mask, sinks)
    o = jnp.einsum('bnkgqm,bnmkd->bnqkgd', p.astype(v.dtype), v_band).reshape(B, S, Q_W)
    w = min(WINDOW, S)
    return o, k[:, S - w:], v[:, S - w:]

def swa_sample(q, k, v, sinks, cache_k, cache_v):
    B, T = q.shape[0], q.shape[1]
    W = cache_k.shape[1]
    k_all = jnp.concatenate([cache_k.astype(k.dtype), k], axis=1)
    v_all = jnp.concatenate([cache_v.astype(v.dtype), v], axis=1)
    qpos = PAST_LEN + jnp.arange(T, dtype=jnp.int32)
    kpos = jnp.concatenate([PAST_LEN - W + jnp.arange(W, dtype=jnp.int32), qpos])
    qg = q.reshape(B, T, N_KV_HEADS, GQA_GROUP, HEAD_DIM)
    s = jnp.einsum('bqkgd,bmkd->bkgqm', qg, k_all).astype(jnp.float32) * (HEAD_DIM ** -0.5)
    mask = window_mask(qpos[:, None], kpos[None, :])
    p = sink_softmax(s, mask, sinks)
    o = jnp.einsum('bkgqm,bmkd->bqkgd', p.astype(v.dtype), v_all).reshape(B, T, Q_W)
    return o, k_all[:, -W:], v_all[:, -W:]

def retention(q, k, v, state0, chunk):
    B, S, H, DK = q.shape
    DV = v.shape[-1]
    nc = S // chunk
    f32 = jnp.float32
    to_chunks = lambda t: t.astype(f32).reshape(B, nc, chunk, H, t.shape[-1]).transpose(1, 0, 3, 2, 4)
    qc, kc, vc = to_chunks(q), to_chunks(k), to_chunks(v)
    log_g = jnp.log(1.0 - 2.0 ** (-5.0 - jnp.arange(H, dtype=f32)))
    i = jnp.arange(chunk, dtype=f32)
    causal = i[:, None] >= i[None, :]
    diff = jnp.where(causal, i[:, None] - i[None, :], 0.0)
    decay_mask = jnp.exp(diff[None] * log_g[:, None, None]) * causal[None]
    q_decay = jnp.exp((i[None, :] + 1.0) * log_g[:, None])[..., None]
    k_decay = jnp.exp((chunk - 1.0 - i[None, :]) * log_g[:, None])[..., None]
    chunk_decay = jnp.exp(chunk * log_g)[:, None, None]

    def step(R, inp):
        qi, ki, vi = inp
        inner = jnp.einsum('bhid,bhjd->bhij', qi, ki) * decay_mask
        o = jnp.einsum('bhij,bhje->bhie', inner, vi) + jnp.einsum('bhid,bhde->bhie', qi * q_decay, R)
        R = R * chunk_decay + jnp.einsum('bhjd,bhje->bhde', ki * k_decay, vi)
        return R, o

    R, o = lax.scan(step, state0.astype(f32), (qc, kc, vc))
    o = o.transpose(1, 0, 3, 2, 4).reshape(B, S, H, DV)
    return o, R

def trunk_layer(x, pos, attn_fn, ret_state0, ret_chunk, ln_g, ln_b, ffn_wi, ffn_wo, w_in, sinks, w_br_attn, w_br_ret, w_o):
    B, S, _ = x.shape
    x = layer_norm(DEEPNORM_ALPHA * x + 0.5 * swiglu(x, ffn_wi[0], ffn_wo[0]), ln_g[0], ln_b[0])
    offs = [int(o) for o in np.cumsum(IN_SPLITS)[:-1]]
    q_a, k_a, v_a, q_r, k_r, v_r, g_r, gate_a, gate_b = jnp.split(x @ w_in, offs, axis=-1)
    fa = attn_inv_freq()
    q_a = rope(q_a.reshape(B, S, N_Q_HEADS, HEAD_DIM), pos, fa)
    k_a = rope(k_a.reshape(B, S, N_KV_HEADS, HEAD_DIM), pos, fa)
    v_a = v_a.reshape(B, S, N_KV_HEADS, HEAD_DIM)
    o_a, new_k, new_v = attn_fn(q_a, k_a, v_a, sinks)
    fr = ret_inv_freq()
    q_r = rope(q_r.reshape(B, S, N_RET_HEADS, RET_KEY_DIM), pos, fr)
    k_r = rope(k_r.reshape(B, S, N_RET_HEADS, RET_KEY_DIM), pos, fr) * (RET_KEY_DIM ** -0.5)
    v_r = v_r.reshape(B, S, N_RET_HEADS, RET_VAL_DIM)
    o_r, new_state = retention(q_r, k_r, v_r, ret_state0, ret_chunk)
    o_r = group_norm(o_r).reshape(B, S, RV_W).astype(x.dtype) * jax.nn.silu(g_r)
    merged = jax.nn.sigmoid(gate_a) * (o_a @ w_br_attn) + jax.nn.sigmoid(gate_b) * (o_r @ w_br_ret)
    x = layer_norm(DEEPNORM_ALPHA * x + merged @ w_o, ln_g[1], ln_b[1])
    x = layer_norm(DEEPNORM_ALPHA * x + 0.5 * swiglu(x, ffn_wi[1], ffn_wo[1]), ln_g[2], ln_b[2])
    return x, new_k, new_v, new_state

def setup_inputs(seed: int = 0) -> dict:
    key = jax.random.key(seed)
    ks = jax.random.split(key, 16)
    f32 = jnp.float32
    W = min(WINDOW, PAST_LEN)
    x_prompt = jax.random.normal(ks[0], (BATCH, SEQ, D_MODEL), f32)
    x_sample = jax.random.normal(ks[1], (DEC_BATCH, DEC_SEQ, D_MODEL), f32)
    cache_k = jax.random.normal(ks[2], (DEPTH, DEC_BATCH, W, N_KV_HEADS, HEAD_DIM), f32)
    cache_v = jax.random.normal(ks[3], (DEPTH, DEC_BATCH, W, N_KV_HEADS, HEAD_DIM), f32) * DEEPNORM_BETA
    state_ret = jax.random.normal(ks[4], (DEPTH, DEC_BATCH, N_RET_HEADS, RET_KEY_DIM, RET_VAL_DIM), f32) * 0.5
    ln_g = 1.0 + 0.02 * jax.random.normal(ks[5], (DEPTH, 3, D_MODEL), f32)
    ln_b = 0.02 * jax.random.normal(ks[6], (DEPTH, 3, D_MODEL), f32)
    ffn_wi = jax.random.normal(ks[7], (DEPTH, 2, D_MODEL, 2 * D_FF), f32) * (D_MODEL ** -0.5)
    ffn_wo = jax.random.normal(ks[8], (DEPTH, 2, D_FF, D_MODEL), f32) * (D_FF ** -0.5) * DEEPNORM_BETA
    col_scale = jnp.concatenate([jnp.full((w,), DEEPNORM_BETA if gi in VALUE_GROUPS else 1.0, f32) for gi, w in enumerate(IN_SPLITS)])
    w_in = jax.random.normal(ks[9], (DEPTH, D_MODEL, N_IN), f32) * (D_MODEL ** -0.5) * col_scale
    attn_sinks = jax.random.normal(ks[10], (DEPTH, N_Q_HEADS), f32)
    w_br_attn = jax.random.normal(ks[11], (DEPTH, Q_W, D_MODEL), f32) * (Q_W ** -0.5)
    w_br_ret = jax.random.normal(ks[12], (DEPTH, RV_W, D_MODEL), f32) * (RV_W ** -0.5)
    w_o = jax.random.normal(ks[13], (DEPTH, D_MODEL, D_MODEL), f32) * (D_MODEL ** -0.5) * DEEPNORM_BETA
    return {'x_prompt': x_prompt, 'x_sample': x_sample, 'cache_k': cache_k, 'cache_v': cache_v,
            'state_ret': state_ret, 'ln_g': ln_g, 'ln_b': ln_b, 'ffn_wi': ffn_wi, 'ffn_wo': ffn_wo,
            'w_in': w_in, 'attn_sinks': attn_sinks, 'w_br_attn': w_br_attn, 'w_br_ret': w_br_ret, 'w_o': w_o}

def reference(x_prompt, x_sample, cache_k, cache_v, state_ret, ln_g, ln_b, ffn_wi, ffn_wo, w_in, attn_sinks, w_br_attn, w_br_ret, w_o):
    B, S, _ = x_prompt.shape
    T = x_sample.shape[1]
    pos_p = jnp.arange(S, dtype=jnp.int32)
    pos_s = PAST_LEN + jnp.arange(T, dtype=jnp.int32)
    y_p, y_s = x_prompt, x_sample
    kp_l, vp_l, rp_l, ks_l, vs_l, rs_l = [], [], [], [], [], []
    for l in range(DEPTH):
        lw = (ln_g[l], ln_b[l], ffn_wi[l], ffn_wo[l], w_in[l], attn_sinks[l], w_br_attn[l], w_br_ret[l], w_o[l])
        zero_state = jnp.zeros((B, N_RET_HEADS, RET_KEY_DIM, RET_VAL_DIM), jnp.float32)
        y_p, kp, vp, rp = trunk_layer(y_p, pos_p, swa_prompt, zero_state, min(RET_CHUNK, S), *lw)
        sample_attn = functools.partial(swa_sample, cache_k=cache_k[l], cache_v=cache_v[l])
        y_s, ks_, vs_, rs_ = trunk_layer(y_s, pos_s, sample_attn, state_ret[l], T, *lw)
        kp_l.append(kp); vp_l.append(vp); rp_l.append(rp)
        ks_l.append(ks_); vs_l.append(vs_); rs_l.append(rs_.astype(state_ret.dtype))
    return (y_p, y_s, jnp.stack(kp_l), jnp.stack(vp_l), jnp.stack(rp_l), jnp.stack(ks_l), jnp.stack(vs_l), jnp.stack(rs_l))


_drawn_inputs = setup_inputs


def setup_inputs(seed=0):
    import zlib

    import numpy as np

    out = dict(_drawn_inputs(seed))
    spreads = {}
    factors = {}
    for name, (base, spread) in spreads.items():
        noise = np.random.default_rng([zlib.crc32(name.encode()), seed]).standard_normal(out[name].shape)
        drawn = base * np.exp(spread * noise) if base else spread * noise
        out[name] = __import__('jax').numpy.asarray(drawn.astype(out[name].dtype))
    for name, factor in factors.items():
        out[name] = (out[name] * factor).astype(out[name].dtype)
    return out
```

```python
from contextlib import ExitStack

import numpy as np

import concourse.bass as bass
from concourse import mybir

F32 = mybir.dt.float32
FR = mybir.dt.float32r
ACT = mybir.ActivationFunctionType
ALU = mybir.AluOpType
AXX = mybir.AxisListType.X

P = 128
D = 1024
KT = D // P
DFF = 2816
NJ = DFF // P
NI = NJ // 2
SEQ, DB, DT = 1024, 8, 8
PAST = 4096
T = SEQ + DB * DT
NT = (T + P - 1) // P
SR = DB * DT
BANK = 512
HQ, HKV, HD = 8, 2, 64
GQ = HQ // HKV
HR, DK, DV = 4, 128, 256
WIN = 128
NG = 3
TG = 3 * P
ALPHA = 2.0 ** 0.25
LN_EPS, GN_EPS = 1e-5, 1e-6
NEG = -1e30
RAW = 3
FSLOTS, MSLOTS = 6, 4
AHEAD_F, AHEAD_M = 4, 3
NP_PHASE = 66
MIX0 = NP_PHASE
FFN2_0 = MIX0 + NG * NP_PHASE
NPIECES = FFN2_0 + NP_PHASE
OFF = {}
_o = 0
for _n, _w in (("qa", 512), ("ka", 128), ("va", 128), ("qr", 512), ("kr", 512), ("vr", 1024), ("gr", 1024),
               ("ga", 1024), ("gb", 1024)):
    OFF[_n] = _o
    _o += _w
CHUNKS = [(0, 384), (384, 384), (768, 320)]
DOWN_BANKS = [5, 6, 7, 3, 4]
LOG_G = np.log(1.0 - 2.0 ** (-5.0 - np.arange(HR)))
CD_PROMPT = [float(np.exp(P * g)) for g in LOG_G]
CD_SAMPLE = [float(np.exp(DT * g)) for g in LOG_G]


def rows_of(t):
    return P if t < NT - 1 else SR


def parts_of(G):
    return [(0, 3, P)] if G < NG - 1 else [(0, 2, P), (2, 1, SR)]


def tokens_of(G):
    return TG if G < NG - 1 else 2 * P + SR


def units_of(G):
    return [(t, n) for t in range(3 if G < NG - 1 else 2) for n in range(HKV)]


def build_timeline(G):
    last = G == NG - 1
    s = [("XT", t) for t in range(3)]
    for h in range(HR):
        s.append(("P", h))
        if h >= 1:
            s.append(("SKV", h - 1))
        if h >= 2:
            s.append(("T", h - 2))
        s.append(("G", h))
        if h >= 1:
            s.append(("PVQ", h - 1))
            if last:
                s.append(("SU", h - 1))
        s.append(("TR", h))
        if h >= 2:
            s.append(("B", h - 2))
    s += [("SKV", 3), ("T", 2), ("GB", 0), ("GB", 1), ("PVQ", 3)]
    if last:
        s.append(("SU", 3))
    s += [("B", 2), ("GB", 2), ("GB", 3), ("GB", 4), ("GB", 5), ("T", 3), ("GB", 6), ("GB", 7), ("B", 3),
          ("MB", 0), ("QA", 0), ("KVA", 0), ("TRK", 0), ("TRQ", 0), ("TRQ", 1), ("TRQ", 2)]
    ga = [("GA", f) for f in range(KT)]
    units = units_of(G)
    if last:
        s.append(("KC", 0))
    for u in range(len(units) + 1):
        if u < len(units):
            s.append(("AS", u))
        if ga:
            s.append(ga.pop(0))
        if u >= 1:
            s.append(("AP", u - 1))
            s.append(("AV", u - 1))
    if last:
        s.append(("SS", 0))
        s += ga[:2]
        ga = ga[2:]
        s += [("SP", 0), ("SV", 0)]
    s += ga
    s += [("A", 0), ("A", 1), ("WO", 0), ("A", 2), ("WO", 1), ("A", 3), ("WO", 2), ("WO", 3)]
    s += [("LN", t) for t in range(3)]
    return s


STAGE_PIECES = {"P": 4, "G": 2, "B": 2, "GB": 1, "GA": 1, "QA": 4, "KVA": 2, "A": 1, "WO": 2}


def numbered_timeline():
    out, n = [], MIX0
    for G in range(NG):
        for kind, x in build_timeline(G):
            out.append((kind, G, x, n))
            n += STAGE_PIECES.get(kind, 0)
        assert n == MIX0 + (G + 1) * NP_PHASE
    return out


TIMELINE = numbered_timeline()


def slot_of(n):
    if n < MIX0:
        return n % FSLOTS
    if n < FFN2_0:
        return (n - MIX0) % MSLOTS
    return (n - FFN2_0 + (FFN2_0 - MIX0) % MSLOTS) % FSLOTS


def last_user(n):
    if n >= FFN2_0 and slot_of(n) >= MSLOTS and n < FFN2_0 + FSLOTS:
        return FFN2_0 - 1
    m = n - 1
    while m >= 0 and slot_of(m) != slot_of(n):
        m -= 1
    return m


def piece_sources(w):
    def cols(src, off, width, k0, nk):
        return src.rearrange("(k p) n -> p k n", p=P)[:, k0:k0 + nk, off:off + width]

    out = [None] * NPIECES
    for G_, kind, x, n in [(G, k, x, n) for k, G, x, n in TIMELINE]:
        for i in range(STAGE_PIECES.get(kind, 0)):
            if kind == "P":
                out[n + i] = [(512, 0, cols(w["w_in"], OFF["qr"] + x * DK, DK, 2 * i, 2)),
                              (512, DK, cols(w["w_in"], OFF["kr"] + x * DK, DK, 2 * i, 2)),
                              (512, 2 * DK, cols(w["w_in"], OFF["vr"] + x * DV, DV, 2 * i, 2))]
            elif kind == "QA":
                out[n + i] = [(512, 0, cols(w["w_in"], OFF["qa"], 512, 2 * i, 2))]
            elif kind == "G":
                out[n + i] = [(256, 0, cols(w["w_in"], OFF["gr"] + x * DV, DV, 4 * i, 4))]
            elif kind == "KVA":
                out[n + i] = [(256, 0, cols(w["w_in"], OFF["ka"], 256, 4 * i, 4))]
            elif kind in ("GA", "GB"):
                out[n + i] = [(P, 0, cols(w["w_in"], OFF[kind.lower()] + x * P, P, 0, KT))]
            elif kind == "B":
                r = x * DV + i * P
                out[n + i] = [(D, 0, w["w_br_ret"][r:r + P, :].rearrange("p (k n) -> p k n", k=1))]
            elif kind == "A":
                out[n + i] = [(256, 0, cols(w["w_br_attn"], x * 256, 256, 0, 4))]
            elif kind == "WO":
                r = (2 * x + i) * P
                out[n + i] = [(D, 0, w["w_o"][r:r + P, :].rearrange("p (k n) -> p k n", k=1))]
    return out


def raw_counts(sources):
    total, out = [0] * RAW, []
    for n in range(NPIECES):
        total[n % RAW] += 16 * (len(sources[n]) if sources[n] else 1)
        out.append(total[n % RAW])
    return out


def hybrid_layer(nc, w, c, o):
    sources = piece_sources(w)
    RAW_AT = raw_counts(sources)

    with ExitStack() as ctx:
        def sem(name):
            return ctx.enter_context(nc.semaphore(name))

        def sb(name, cols, dt=F32, stack=ctx):
            return stack.enter_context(nc.sbuf_tensor(name, [P, cols], dt))

        y = sb("y", NT * D)
        raw = sb("raw", RAW * D)
        w_hi4, w_lo4 = sb("w_hi4", MSLOTS * D, FR), sb("w_lo4", MSLOTS * D, FR)
        ident = sb("ident", P)
        ln_g, ln_b = sb("ln_g_rows", D), sb("ln_b_rows", D)
        ret_mask = sb("ret_mask", HR * P)
        ret_mask_s = sb("ret_mask_s", HR * SR)
        kdec_t, qdec_t = sb("kdec_t", 2 * HR), sb("qdec_t", 2 * HR)
        att_mask = sb("att_mask", 2 * 2 * WIN)
        att_mask_s = sb("att_mask_s", 2 * 192)
        batch_cols = sb("batch_cols", DB * SR)
        batch_rows = sb("batch_rows", DB)
        sinks, sinks_s = sb("sinks", HQ), sb("sinks_s", HKV)
        cs_att = sb("cs_att", 3 * 2 * 32)
        cs_ret = sb("cs_ret", 3 * 2 * 64)
        neg_half = sb("neg_half", 4)
        st6, mv = sb("ln_stats", NT * 12), sb("ln_mv", NT * 2)
        ve, rs, nmr = sb("ln_ve", NT), sb("ln_rs", NT), sb("ln_nmr", NT)
        gst, gmv = sb("gn_stats", 18), sb("gn_mv", 6)
        gve, grs = sb("gn_ve", 3), sb("gn_rs", 3)
        mx, nmx, esd, es, rsum, den, rden = [sb(n, 8) for n in ("mx", "nmx", "esd", "es", "rsum", "den", "rden")]
        ps = ctx.enter_context(nc.psum_tensor("ps", [P, 8 * BANK], F32))

        with ExitStack() as f:
            w_hi2, w_lo2 = sb("w_hi2", 2 * D, FR, f), sb("w_lo2", 2 * D, FR, f)
            xT_hi, xT_lo = sb("xT_hi", KT * T, FR, f), sb("xT_lo", KT * T, FR, f)
            h_hi, h_lo = sb("h_hi", 2 * T, FR, f), sb("h_lo", 2 * T, FR, f)
            hs = sb("hs", T, F32, f)
        m = ctx.enter_context(ExitStack())
        xg_hi, xg_lo = sb("xg_hi", KT * TG, FR, m), sb("xg_lo", KT * TG, FR, m)
        racc = sb("racc", KT * TG, F32, m)
        sig = sb("sig", KT * TG, F32, m)
        rst = sb("rst", 5 * DV, F32, m)
        ka_prev, va_prev = sb("ka_prev", P, F32, m), sb("va_prev", P, F32, m)
        tA, tB = sb("tA", 512, F32, m), sb("tB", 512, F32, m)
        with ExitStack() as r:
            qk = sb("qk", 3 * 2 * DK, F32, r)
            kdec = sb("kdec", 2 * 3 * DK, F32, r)
            v_r = sb("v_r", 2 * 3 * DV, F32, r)
            gs = sb("gs", 2 * 3 * DV, F32, r)
            qT, kT = sb("qT", TG, F32, r), sb("kT", TG, F32, r)
            pt_r = sb("pt_r", TG, F32, r)
            r12 = sb("r12", 2 * DV, F32, r)
            orow = sb("orow", 3 * DV, F32, r)
            orT_hi, orT_lo = sb("orT_hi", 2 * TG, FR, r), sb("orT_lo", 2 * TG, FR, r)
            st = sb("st", DB * DV, F32, r)
            kdec_m = sb("kdec_m", 4 * DK, F32, r)
            qT_m = sb("qT_m", DB * SR, F32, r)
        with ExitStack() as a:
            qa = sb("qa", 2 * 512, F32, a)
            ka = sb("ka", 3 * P, F32, a)
            qaT = sb("qaT", 3 * 512, F32, a)
            kaT, va = sb("kaT", 4 * P, F32, a), sb("va", 4 * P, F32, a)
            oaT_hi, oaT_lo = sb("oaT_hi", 4 * TG, FR, a), sb("oaT_lo", 4 * TG, FR, a)
            kcT, vc = sb("kcT", DB * P, F32, a), sb("vc", DB * P, F32, a)
            with ExitStack() as a1:
                prob = sb("prob", 2 * 1024, F32, a1)
                probT = sb("probT", 1024, F32, a1)
            mT_hi, mT_lo = sb("mT_hi", 4 * TG, FR, a), sb("mT_lo", 4 * TG, FR, a)

        raw_loaded = [sem(f"raw_loaded{i}") for i in range(RAW)]
        hi_ready, lo_ready = sem("hi_ready"), sem("lo_ready")
        piece_used = sem("piece_used")
        x_loaded = [sem(f"x_loaded{t}") for t in range(NT)]
        const_loaded = sem("const_loaded")
        ln_rows_loaded = sem("ln_rows_loaded")
        cs_loaded = sem("cs_loaded")
        xt_done, xT_hi_ready, xT_lo_ready = sem("xt_done"), sem("xT_hi_ready"), sem("xT_lo_ready")
        y_scaled = sem("y_scaled")
        silu_done, h_mul, h_hi_ready, h_lo_ready = [sem(n) for n in ("silu_done", "h_mul", "h_hi_ready", "h_lo_ready")]
        down_done, acc_done = sem("down_done"), sem("acc_done")
        ln_aggr, ln_rstd, ln_hat, ln_affine = [sem(n) for n in ("ln_aggr", "ln_rstd", "ln_hat", "ln_affine")]
        dve_step, pool_step, act_step = sem("dve_step"), sem("pool_step"), sem("act_step")
        rope_read, v_ready, qk_ready, kdec_ready = [sem(n) for n in ("rope_read", "v_ready", "qk_ready", "kdec_ready")]
        gs_ready, tr_done, qkT_ready = sem("gs_ready"), sem("tr_done"), sem("qkT_ready")
        s_done, pt_ready, kv_done, r_ready = sem("s_done"), sem("pt_ready"), sem("kv_done"), sem("r_ready")
        pvq_done, o_ready, gn_aggr, gn_rstd, gn_done = [sem(n) for n in ("pvq_done", "o_ready", "gn_aggr", "gn_rstd", "gn_done")]
        t_done, or_hi_ready, or_lo_ready = sem("t_done"), sem("or_hi_ready"), sem("or_lo_ready")
        b_done, racc_done, sig_done, mb_done = sem("b_done"), sem("racc_done"), sem("sig_done"), sem("mb_done")
        st_loaded, qTm_ready, kdm_ready, su_done, st_ready, st_stored = [
            sem(n) for n in ("st_loaded", "qTm_ready", "kdm_ready", "su_done", "st_ready", "st_stored")]
        va_ready, ka_ready, trk_done, kaT_ready = [sem(n) for n in ("va_ready", "ka_ready", "trk_done", "kaT_ready")]
        qa_ready, trq_done, qaT_ready = sem("qa_ready"), sem("trq_done"), sem("qaT_ready")
        as_done, sm_read, nmx_ready, exp_done, p_ready = [sem(n) for n in ("as_done", "sm_read", "nmx_ready", "exp_done", "p_ready")]
        ap_done, pT_ready, av_done, oa_hi_ready, oa_lo_ready = [
            sem(n) for n in ("ap_done", "pT_ready", "av_done", "oa_hi_ready", "oa_lo_ready")]
        kc_loaded, vc_loaded, kc_tr, kcT_ready = sem("kc_loaded"), sem("vc_loaded"), sem("kc_tr"), sem("kcT_ready")
        m_ready, m_hi_ready, m_lo_ready = sem("m_ready"), sem("m_hi_ready"), sem("m_lo_ready")
        wo_done, wacc_done = sem("wo_done"), sem("wacc_done")
        prev_zeroed = sem("prev_zeroed")
        out_stored = sem("out_stored")
        y_stored = sem("y_stored")

        def wslot(n, lo):
            s = slot_of(n)
            if s < MSLOTS:
                return (w_lo4 if lo else w_hi4)[:, s * D:(s + 1) * D]
            return (w_lo2 if lo else w_hi2)[:, (s - MSLOTS) * D:(s - MSLOTS + 1) * D]

        def fr(ap):
            return ap.bitcast(F32)

        def y_tile(t):
            return y[0:rows_of(t), t * D:(t + 1) * D]

        def bank(b, rows=P, off=0, n=BANK):
            return ps[0:rows, b * BANK + off:b * BANK + off + n]

        def split_hi(eng, n, i=0, step=0):
            eng.wait_ge(raw_loaded[n % RAW], RAW_AT[n] + 16 * (step // RAW) * i)
            before = n - FSLOTS if step else last_user(n)
            if step or before >= 0:
                eng.wait_ge(piece_used, before + 1 + step * i)
            s = n % RAW
            nc.scalar.activation(wslot(n, False), raw[:, s * D:(s + 1) * D], ACT.Copy).then_inc(hi_ready, 1)

        def split_lo(eng, n, i=0, step=0):
            eng.wait_ge(hi_ready, n + 1 + step * i)
            s = n % RAW
            nc.vector.tensor_tensor(wslot(n, True), raw[:, s * D:(s + 1) * D], fr(wslot(n, False)),
                                    ALU.subtract).then_inc(lo_ready, 1)

        class Pace:
            def __init__(self, eng, split, start):
                self.eng, self.split, self.n = eng, split, start

            def upto(self, n):
                while self.n < min(n, NPIECES):
                    self.split(self.eng, self.n)
                    self.n += 1

            def stage(self, first, count):
                ahead = AHEAD_M if first + count < FFN2_0 - 3 else 2
                held = count if count == 2 else 1
                self.upto(first + count + ahead - held + 1 if count != 2 else first + 2 + MSLOTS - 2)

        block = ctx.enter_context(nc.Block())

        @block.sync
        def _(sp):
            for t in range(NT):
                src = w["x_prompt"][0, t * P:(t + 1) * P, :] if t < NT - 1 else w["x_sample"].rearrange("b t d -> (b t) d")
                sp.dma_start(y_tile(t), src).then_inc(x_loaded[t], 16)

            def raw_free(n, i=0, step=0):
                if step or n >= RAW:
                    sp.wait_ge(lo_ready, n - RAW + 1 + step * i)

            def load_ffn(f, base, i, peeled):
                wi = w["ffn_wi"][0, f].rearrange("(k p) n -> p k n", p=P)
                wo = w["ffn_wo"][0, f]
                step = 0 if peeled else 6
                todo = [(0, DFF), (1, 0), (1, DFF), (2, 0)] + [(0, None), (1, None)]
                n = base + 1 + (6 * i if peeled else 0)
                for dj, off in todo:
                    if off == 0 and dj == 2 and peeled and i == NI - 1:
                        continue
                    raw_free(n, i, step)
                    s = n % RAW
                    dst = raw[:, s * D:(s + 1) * D]
                    j = i * 2 + dj
                    if off is None:
                        sp.dma_start(dst, wo[j * P:(j + 1) * P, :] if peeled else wo[bass.ds(j * P, P), :])\
                          .then_inc(raw_loaded[s], 16)
                    else:
                        src = wi[:, :, off + j * P:off + (j + 1) * P] if peeled else wi[:, :, bass.ds(j * P + off, P)]
                        sp.dma_start(dst.rearrange("p (k n) -> p k n", k=KT), src).then_inc(raw_loaded[s], 16)
                    n += 1

            def load_ffn_phase(f, base):
                wi = w["ffn_wi"][0, f].rearrange("(k p) n -> p k n", p=P)
                raw_free(base)
                sp.dma_start(raw[:, 0:D].rearrange("p (k n) -> p k n", k=KT), wi[:, :, 0:P]).then_inc(raw_loaded[0], 16)
                load_ffn(f, base, 0, True)
                with sp.Fori(1, NI - 1) as i:
                    load_ffn(f, base, i, False)
                load_ffn(f, base, NI - 1, True)

            load_ffn_phase(0, 0)
            for n in range(MIX0, FFN2_0):
                raw_free(n)
                s = n % RAW
                for width, off, src in sources[n]:
                    k, cols = src.shape[1], src.shape[2]
                    dst = raw[:, s * D:(s + 1) * D].rearrange("p (k n) -> p k n", n=width)[:, 0:k, off:off + cols]
                    sp.dma_start(dst, src).then_inc(raw_loaded[s], 16)
            load_ffn_phase(1, FFN2_0)
            for t in range(NT):
                sp.wait_ge(ln_affine, 2 * NT + t + 1)
                dst = o["y_prompt"][0, t * P:(t + 1) * P, :] if t < NT - 1 else o["y_sample"].rearrange("b t d -> (b t) d")
                sp.dma_start(dst, y_tile(t)).then_inc(y_stored, 16)
            sp.wait_ge(y_stored, 16 * NT)

        @block.gpsimd
        def _(pool):
            step = [0]

            def link(ins):
                step[0] += 1
                ins.then_inc(pool_step, 1)
                pool.wait_ge(pool_step, step[0])

            link(nc.gpsimd.memset(neg_half[:], -0.5))
            nc.gpsimd.memset(ka_prev[:], 0.0) if False else None
            n_out = [0]

            def store(dst, src):
                pool.dma_start(dst, src).then_inc(out_stored, 16)
                n_out[0] += 1

            keep = WIN - DT
            for name, cache in (("kcs", "cache_k"), ("vcs", "cache_v")):
                store(o[name][0, :, 0:keep].rearrange("b w n d -> b (w n d)"),
                      w[cache][0, :, DT:WIN].rearrange("b w n d -> b (w n d)"))

            def load_ln_rows(k):
                if k:
                    pool.wait_ge(pool_step, step[0])
                pool.dma_start(ln_g[:], w["ln_g"][0, k:k + 1, :].to_broadcast([P, D])).then_inc(ln_rows_loaded, 16)
                pool.dma_start(ln_b[:], w["ln_b"][0, k:k + 1, :].to_broadcast([P, D])).then_inc(ln_rows_loaded, 16)

            load_ln_rows(0)

            def rstd(idx, t):
                R = rows_of(t)
                pool.wait_ge(ln_aggr, idx + 1)
                link(nc.gpsimd.tensor_scalar(ve[0:R, t:t + 1], mv[0:R, 2 * t + 1:2 * t + 2], LN_EPS, None, ALU.add))
                link(nc.gpsimd.tensor_tensor(rs[0:R, t:t + 1], ve[0:R, t:t + 1], neg_half[0:R, 0:1], ALU.pow))
                nc.gpsimd.tensor_scalar(nmr[0:R, t:t + 1], mv[0:R, 2 * t:2 * t + 1], rs[0:R, t:t + 1], -1.0,
                                        ALU.mult, ALU.mult).then_inc(ln_rstd, 1)

            def affine(idx, t, k):
                R = rows_of(t)
                pool.wait_ge(ln_rows_loaded, 32 * (k + 1))
                pool.wait_ge(ln_hat, idx + 1)
                link(nc.gpsimd.tensor_tensor(y_tile(t), y_tile(t), ln_g[0:R, :], ALU.mult))
                nc.gpsimd.tensor_tensor(y_tile(t), y_tile(t), ln_b[0:R, :], ALU.add).then_inc(ln_affine, 1)

            def scale_y(v, t):
                pool.wait_ge(xt_done, v + 1)
                nc.gpsimd.tensor_scalar(y_tile(t), y_tile(t), ALPHA, None, ALU.mult).then_inc(y_scaled, 1)

            def ln_all(k):
                for t in range(NT + 1):
                    if t < NT:
                        rstd(k * NT + t, t)
                    if t >= 1:
                        affine(k * NT + t - 1, t - 1, k)

            for t in range(NT):
                scale_y(t, t)
            ln_all(0)
            for kind, G, x, n in TIMELINE:
                g = HR * G + x
                if kind == "XT":
                    if x == 0:
                        if G:
                            pool.wait_ge(qa_ready, 3 * G)
                        pool.dma_start(cs_att[:], c["cs_att"][:, G]).then_inc(cs_loaded, 16)
                        pool.dma_start(cs_ret[:], c["cs_ret"][:, G]).then_inc(cs_loaded, 16)
                        if G == 0:
                            pool.wait_ge(ln_affine, NT)
                            load_ln_rows(1)
                        if G == NG - 1:
                            pool.wait_ge(piece_used, MIX0 + G * NP_PHASE)
                            pool.dma_start(st[:].rearrange("p (b e) -> p b e", b=DB),
                                           w["state_ret"][0, :, 0].rearrange("b p e -> p b e")).then_inc(st_loaded, 16)
                    scale_y(NT + 3 * G + x, 3 * G + x)
                elif kind == "PVQ":
                    pool.wait_ge(gn_aggr, g + 1)
                    for i, (t0, nt, R) in enumerate(parts_of(G)):
                        link(nc.gpsimd.tensor_scalar(gve[0:R, t0:t0 + nt],
                                                     gmv[0:R, :].rearrange("p (t s) -> p t s", s=2)[:, t0:t0 + nt, 1],
                                                     GN_EPS, None, ALU.add))
                        for t in range(t0, t0 + nt):
                            ins = nc.gpsimd.tensor_tensor(grs[0:R, t:t + 1], gve[0:R, t:t + 1], neg_half[0:R, 0:1], ALU.pow)
                    ins.then_inc(gn_rstd, 1)
                elif kind == "SU":
                    pool.wait_ge(st_ready, 2 * (x + 1))
                    pool.dma_start(o["rs"][0, :, x].rearrange("b p e -> p b e"),
                                   st[:].rearrange("p (b e) -> p b e", b=DB)).then_inc(st_stored, 16)
                    if x < HR - 1:
                        pool.wait_ge(st_stored, 16 * (x + 1))
                        pool.dma_start(st[:].rearrange("p (b e) -> p b e", b=DB),
                                       w["state_ret"][0, :, x + 1].rearrange("b p e -> p b e")).then_inc(st_loaded, 16)
                    slot = (x - NG) % 5
                    store(o["rp"][0, 0, x], rst[:, slot * DV:(slot + 1) * DV])
                elif kind == "QA" and G == NG - 1:
                    pool.wait_ge(piece_used, n)
                    pool.wait_ge(st_stored, 16 * HR)
                    pool.dma_start(prob[:, 0:1024].rearrange("p (b e) -> p b e", b=DB),
                                   w["cache_k"][0].rearrange("b w n d -> w b (n d)")).then_inc(kc_loaded, 16)
                    pool.dma_start(vc[:].rearrange("p (b e) -> p b e", b=DB),
                                   w["cache_v"][0].rearrange("b w n d -> w b (n d)")).then_inc(vc_loaded, 16)
                elif kind == "TRK" and G == NG - 1:
                    pool.wait_ge(ka_ready, NG)
                    pool.wait_ge(va_ready, NG)
                    store(o["kcp"][0, 0].rearrange("w n d -> w (n d)"), ka[:, P:2 * P])
                    store(o["vcp"][0, 0].rearrange("w n d -> w (n d)"), va[:, 2 * P:3 * P])
                    for b in range(DB):
                        store(o["kcs"][0, b, keep:WIN].rearrange("w n d -> w (n d)"), ka[b * DT:(b + 1) * DT, 2 * P:3 * P])
                        store(o["vcs"][0, b, keep:WIN].rearrange("w n d -> w (n d)"), va[b * DT:(b + 1) * DT, 3 * P:4 * P])
                elif kind == "LN":
                    t = 3 * G + x
                    rstd(NT + t, t)
                    affine(NT + t, t, 1)
            for t in range(NT):
                scale_y(2 * NT + t, t)
            pool.wait_ge(ln_affine, 2 * NT)
            load_ln_rows(2)
            ln_all(2)
            pool.wait_ge(out_stored, 16 * n_out[0])
            pool.wait_ge(st_stored, 16 * HR)

        @block.scalar
        def _(act):
            consts = [(ident, c["ident"]), (ret_mask, c["ret_mask"]), (kdec_t, c["kdec_t"]), (qdec_t, c["qdec_t"]),
                      (att_mask, c["att_mask"]), (att_mask_s, c["att_mask_s"]), (batch_cols, c["batch_cols"]),
                      (sinks, c["sinks"]), (sinks_s, c["sinks_s"])]
            for dst, src in consts:
                act.dma_start(dst[:], src).then_inc(const_loaded, 16)
            for dst, src in ((ret_mask_s, c["ret_mask_s"]), (batch_rows, c["batch_rows"])):
                act.dma_start(dst[0:SR, :], src).then_inc(const_loaded, 16)

            def xT_evac(v, t, dst, width, col):
                R = rows_of(t)
                act.wait_ge(xt_done, v + 1)
                pair = ps[:, (3 if v % 2 else 0) * BANK:][:, 0:KT * P].rearrange("p (k c) -> p k c", k=KT)[:, :, 0:R]
                out = dst[:].rearrange("p (k c) -> p k c", c=width)[:, :, col:col + R]
                nc.scalar.activation(out, pair, ACT.Copy).then_inc(xT_hi_ready, 1)

            def hat(idx, t):
                R = rows_of(t)
                act.wait_ge(ln_rstd, idx + 1)
                nc.scalar.activation(y_tile(t), y_tile(t), ACT.Identity, bias=nmr[0:R, t:t + 1],
                                     scale=rs[0:R, t:t + 1]).then_inc(ln_hat, 1)

            def ffn(f, base):
                J0, I0 = NJ * f, NI * f

                def silu(jexpr, n, i, st):
                    act.wait_ge(piece_used, n + 1 + st * i)
                    if not (isinstance(jexpr, int) and jexpr == 0):
                        act.wait_ge(h_lo_ready, jexpr * 3)
                    for ci, (c0, cw) in enumerate(CHUNKS):
                        nc.scalar.activation(hs[:, c0:c0 + cw], bank(ci, n=cw), ACT.Silu).then_inc(silu_done, 1)

                def h_round(jexpr, slot, prior):
                    if prior is not None:
                        act.wait_ge(piece_used, prior)
                    for ci, (c0, cw) in enumerate(CHUNKS):
                        act.wait_ge(h_mul, jexpr * 3 + ci + 1)
                        nc.scalar.activation(h_hi[:, slot * T + c0:slot * T + c0 + cw], hs[:, c0:c0 + cw],
                                             ACT.Copy).then_inc(h_hi_ready, 1)

                def turn(i, peeled):
                    st = 0 if peeled else 6
                    n = base + 1 + (6 * i if peeled else 0)
                    J = i * 2 + J0
                    lastt = peeled and i == NI - 1

                    def split(k):
                        if not peeled:
                            split_hi(act, n + k + AHEAD_F, i, 6)
                        else:
                            pace.upto(n + k + AHEAD_F + 1)
                    prior = None if (peeled and i == 0) else (base + 1 + 6 * i)
                    split(0)
                    h_round(J, 0, prior)
                    split(1)
                    silu(J + 1, n + 1, i, st)
                    split(2)
                    h_round(J + 1, 1, prior)
                    split(3)
                    if not lastt:
                        silu(J + 2, n + 3, i, st)
                        split(4)
                        split(5)

                pace.upto(base + AHEAD_F + 1)
                silu(J0, base, 0, 0)
                turn(0, True)
                with act.Fori(1, NI - 1) as i:
                    turn(i, False)
                pace.n = base + 1 + 6 * (NI - 1) + AHEAD_F
                turn(NI - 1, True)

            pace = Pace(act, split_hi, 0)
            act.wait_ge(const_loaded, 16 * (len(consts) + 2))
            pace.upto(AHEAD_F)
            for t in range(NT):
                xT_evac(t, t, xT_hi, T, t * P)
            ffn(0, 0)
            for t in range(NT):
                hat(t, t)

            chain = [0]

            def link(ins):
                chain[0] += 1
                ins.then_inc(act_step, 1)
                act.wait_ge(act_step, chain[0])

            n_unit = [0]
            n_tile = [0]
            for kind, G, x, n in TIMELINE:
                g = HR * G + x
                TGn = tokens_of(G)
                k = STAGE_PIECES.get(kind, 0)
                if k:
                    pace.stage(n, k)
                if kind == "XT":
                    xT_evac(NT + 3 * G + x, 3 * G + x, xg_hi, TG, x * P)
                elif kind == "P":
                    act.wait_ge(rope_read, g + 1)
                    if g >= 2:
                        act.wait_ge(pvq_done, g - 1)
                        if G == NG - 1 and x >= 2:
                            act.wait_ge(su_done, 2 * (x - 1))
                    for t0, nt, R in parts_of(G):
                        src = ps[0:R, 0:3 * BANK].rearrange("p (t c) -> p t c", t=3)[:, t0:t0 + nt, 2 * DK:]
                        dst = v_r[0:R, (g % 2) * 3 * DV:(g % 2 + 1) * 3 * DV].rearrange("p (t c) -> p t c", t=3)[:, t0:t0 + nt, :]
                        ins = nc.scalar.activation(dst, src, ACT.Copy)
                    ins.then_inc(v_ready, 1)
                elif kind == "G":
                    act.wait_ge(piece_used, n + 2)
                    if g >= 2:
                        act.wait_ge(gn_done, g - 1)
                    for t0, nt, R in parts_of(G):
                        src = ps[0:R, 3 * BANK:6 * BANK].rearrange("p (t c) -> p t c", t=3)[:, t0:t0 + nt, 0:DV]
                        dst = gs[0:R, (g % 2) * 3 * DV:(g % 2 + 1) * 3 * DV].rearrange("p (t c) -> p t c", t=3)[:, t0:t0 + nt, :]
                        ins = nc.scalar.activation(dst, src, ACT.Silu)
                    ins.then_inc(gs_ready, 1)
                elif kind == "TR":
                    act.wait_ge(tr_done, g + 1)
                    nc.scalar.activation(qT[:, 0:TGn], bank(6, n=TGn), ACT.Copy).then_inc(qkT_ready, 1)
                    nc.scalar.activation(kT[:, 0:TGn], bank(7, n=TGn), ACT.Copy).then_inc(qkT_ready, 1)
                elif kind == "PVQ":
                    act.wait_ge(pvq_done, g + 1)
                    if g:
                        act.wait_ge(t_done, g)
                    for i, (t0, nt, R) in enumerate(parts_of(G)):
                        ins = nc.scalar.activation(orow[0:R, t0 * DV:(t0 + nt) * DV],
                                                   ps[0:R, 6 * BANK + t0 * DV:6 * BANK + (t0 + nt) * DV], ACT.Copy,
                                                   scale=qdec_t[0:R, HR * i + x:HR * i + x + 1])
                    ins.then_inc(o_ready, 1)
                elif kind == "T":
                    act.wait_ge(t_done, g + 1)
                    src = ps[:, 6 * BANK:8 * BANK].rearrange("p (e c) -> p e c", e=2)[:, :, 0:TGn]
                    dst = orT_hi[:].rearrange("p (e c) -> p e c", e=2)[:, :, 0:TGn]
                    nc.scalar.activation(dst, src, ACT.Copy).then_inc(or_hi_ready, 1)
                elif kind in ("GB", "GA"):
                    act.wait_ge(piece_used, n + 1)
                    b = x % 3 if kind == "GB" else 6 + x % 2
                    if kind == "GA":
                        act.wait_ge(mb_done, KT * G + x + 1)
                    elif G:
                        act.wait_ge(m_ready, KT * G)
                    nc.scalar.activation(sig[:, x * TG:x * TG + TGn], bank(b, n=TGn), ACT.Sigmoid).then_inc(sig_done, 1)
                elif kind == "KVA":
                    act.wait_ge(ka_ready, G + 1)
                    if G == 0:
                        act.wait_ge(prev_zeroed, 2)
                    link(nc.scalar.activation(va[:, 0:P], va_prev[:], ACT.Copy))
                    for t0, nt, R in parts_of(G):
                        src = ps[0:R, 3 * BANK:6 * BANK].rearrange("p (t c) -> p t c", t=3)[:, t0:t0 + nt, P:2 * P]
                        dst = va[0:R, P:].rearrange("p (t c) -> p t c", t=3)[:, t0:t0 + nt, :]
                        ins = nc.scalar.activation(dst, src, ACT.Copy)
                    ins.then_inc(va_ready, 1)
                    if G < NG - 1:
                        act.wait_ge(va_ready, G + 1)
                        link(nc.scalar.activation(va_prev[:], va[:, 3 * P:4 * P], ACT.Copy))
                elif kind == "TRK":
                    act.wait_ge(trk_done, G + 1)
                    link(nc.scalar.activation(kaT[:, 0:P], ka_prev[:], ACT.Copy))
                    nc.scalar.activation(kaT[:, P:P + TGn], bank(7, n=TGn), ACT.Copy).then_inc(kaT_ready, 1)
                    if G < NG - 1:
                        act.wait_ge(kaT_ready, G + 1)
                        link(nc.scalar.activation(ka_prev[:], kaT[:, 3 * P:4 * P], ACT.Copy))
                elif kind == "TRQ":
                    R = rows_of(3 * G + x)
                    act.wait_ge(trq_done, 3 * G + x + 1)
                    src = bank(5).rearrange("p (g c) -> p g c", g=GQ)[:, :, 0:R]
                    if R == P:
                        dst = qaT[:, x * 512:(x + 1) * 512].rearrange("p (g c) -> p g c", g=GQ)
                    else:
                        src = src.rearrange("p g (b t) -> p g b t", b=DB)
                        dst = qaT[:, x * 512:x * 512 + GQ * SR].rearrange("p (b g t) -> p g b t", b=DB, g=GQ)
                    nc.scalar.activation(dst, src, ACT.Copy).then_inc(qaT_ready, 1)
                elif kind == "KC":
                    act.wait_ge(kc_tr, 1)
                    nc.scalar.activation(kcT[:], ps[:, 6 * BANK:8 * BANK], ACT.Copy).then_inc(kcT_ready, 1)
                elif kind in ("AS", "SS"):
                    u = n_unit[0]
                    act.wait_ge(nmx_ready, u + 1)
                    nc.scalar.activation(es[:, 0:4], esd[:, 0:4], ACT.Exp)
                    wd = 2 * WIN if kind == "AS" else 192
                    pb = prob[:, (u % 2) * 1024:(u % 2) * 1024 + 4 * wd]
                    for q in range(4):
                        ins = nc.scalar.activation(pb[:, q * wd:(q + 1) * wd], pb[:, q * wd:(q + 1) * wd], ACT.Exp,
                                                   bias=nmx[:, q:q + 1], accum_out=rsum[:, q:q + 1])
                    ins.then_inc(exp_done, 1)
                    n_unit[0] += 1
                elif kind in ("AP", "SP"):
                    u = n_unit[0] if kind == "SP" else (len(units_of(0)) * G + x + 1)
                    act.wait_ge(ap_done, u)
                    if u >= 2:
                        act.wait_ge(av_done, u - 1)
                    if kind == "AP":
                        nc.scalar.activation(probT[:], ps[:, 0:2 * BANK], ACT.Copy).then_inc(pT_ready, 1)
                    else:
                        nc.scalar.activation(probT[:, 0:512], bank(0), ACT.Copy)
                        nc.scalar.activation(probT[0:SR, 512:1024], bank(1, SR), ACT.Copy).then_inc(pT_ready, 1)
                elif (kind == "AV" and x % 2 == 1) or kind == "SV":
                    u = len(units_of(0)) * G + x + 1 if kind == "AV" else len(units_of(0)) * G + 5
                    t = x // 2 if kind == "AV" else 2
                    R = rows_of(3 * G + t)
                    act.wait_ge(av_done, u)
                    nc.scalar.activation(oaT_hi[:].rearrange("p (k c) -> p k c", k=4)[:, :, t * P:t * P + R],
                                         bank(2).rearrange("p (k c) -> p k c", k=4)[:, :, 0:R], ACT.Copy).then_inc(oa_hi_ready, 1)
                elif kind == "A":
                    act.wait_ge(m_ready, KT * G + 2 * x + 2)
                    if x >= 2:
                        wo_n = [nn for kk, gg, xx, nn in TIMELINE if (kk, gg, xx) == ("WO", G, x - 2)][0]
                        act.wait_ge(piece_used, wo_n + 2)
                    src = sig[:, 2 * x * TG:(2 * x + 2) * TG].rearrange("p (f c) -> p f c", f=2)[:, :, 0:TGn]
                    dst = mT_hi[:, (x % 2) * 2 * TG:(x % 2 + 1) * 2 * TG].rearrange("p (f c) -> p f c", f=2)[:, :, 0:TGn]
                    nc.scalar.activation(dst, src, ACT.Copy).then_inc(m_hi_ready, 1)
                elif kind == "LN":
                    hat(NT + 3 * G + x, 3 * G + x)

            act.wait_ge(st_stored, 16 * HR)
            act.wait_ge(out_stored, 16 * (2 + HR + 2 + 2 * DB))
            for t in range(NT):
                xT_evac(2 * NT + t, t, xT_hi, T, t * P)
            ffn(1, FFN2_0)
            for t in range(NT):
                hat(2 * NT + t, t)

        @block.vector
        def _(dve):
            step = [0]

            def link(ins):
                step[0] += 1
                ins.then_inc(dve_step, 1)
                dve.wait_ge(dve_step, step[0])

            tt = nc.vector.tensor_tensor

            def xT_evac(v, t, dst_hi, dst_lo, width, col):
                R = rows_of(t)
                dve.wait_ge(xT_hi_ready, v + 1)
                pair = ps[:, (3 if v % 2 else 0) * BANK:][:, 0:KT * P].rearrange("p (k c) -> p k c", k=KT)[:, :, 0:R]
                hi = fr(dst_hi[:].rearrange("p (k c) -> p k c", c=width)[:, :, col:col + R])
                lo = dst_lo[:].rearrange("p (k c) -> p k c", c=width)[:, :, col:col + R]
                tt(lo, pair, hi, ALU.subtract).then_inc(xT_lo_ready, 1)

            def ln_stats(t):
                R = rows_of(t)
                for q in range(2):
                    ins = nc.vector.bn_stats(st6[0:R, 12 * t + 6 * q:12 * t + 6 * q + 6],
                                             y[0:R, t * D + 512 * q:t * D + 512 * q + 512])
                link(ins)
                nc.vector.bn_aggr(mv[0:R, 2 * t:2 * t + 2], st6[0:R, 12 * t:12 * t + 12]).then_inc(ln_aggr, 1)

            def ffn(f, base):
                J0, I0 = NJ * f, NI * f

                def mul(jexpr, n, i, st_):
                    dve.wait_ge(piece_used, n + 1 + st_ * i)
                    for ci, (c0, cw) in enumerate(CHUNKS):
                        dve.wait_ge(silu_done, jexpr * 3 + ci + 1)
                        nc.vector.scalar_tensor_tensor(out=hs[:, c0:c0 + cw], in0=hs[:, c0:c0 + cw], scalar=0.5,
                                                       in1=bank(3 + ci, n=cw), op0=ALU.mult, op1=ALU.mult)\
                            .then_inc(h_mul, 1)

                def h_rest(jexpr, slot):
                    for ci, (c0, cw) in enumerate(CHUNKS):
                        dve.wait_ge(h_hi_ready, jexpr * 3 + ci + 1)
                        hi = h_hi[:, slot * T + c0:slot * T + c0 + cw]
                        tt(h_lo[:, slot * T + c0:slot * T + c0 + cw], hs[:, c0:c0 + cw], fr(hi), ALU.subtract)\
                            .then_inc(h_lo_ready, 1)

                def accumulate(i, n_wo, st_, first, stats):
                    for q in range(2 * NT):
                        t, half = q // 2, q % 2
                        R = rows_of(t)
                        if first and half == 0:
                            dve.wait_ge(y_scaled, 2 * NT * f + t + 1)
                        if q < 2 * NT - 1:
                            dve.wait_ge(down_done, i * 17 + I0 * 17 + q + 1)
                        else:
                            dve.wait_ge(piece_used, n_wo + 2 + st_ * i)
                        ysl = y[0:R, t * D + half * 512:t * D + half * 512 + 512]
                        tt(ysl, ysl, bank(DOWN_BANKS[q % 5], R), ALU.add).then_inc(acc_done, 1)
                        if stats and half == 1:
                            dve.wait_ge(acc_done, 18 * (I0 + i) + q + 1)
                            ln_stats(t)

                def turn(i, peeled):
                    st_ = 0 if peeled else 6
                    n = base + 1 + (6 * i if peeled else 0)
                    J = i * 2 + J0
                    lastt = peeled and i == NI - 1

                    def split(k):
                        if not peeled:
                            split_lo(dve, n + k + AHEAD_F, i, 6)
                        else:
                            pace.upto(n + k + AHEAD_F + 1)
                    split(0)
                    mul(J, n, i, st_)
                    h_rest(J, 0)
                    split(1)
                    split(2)
                    mul(J + 1, n + 2, i, st_)
                    h_rest(J + 1, 1)
                    split(3)
                    if not lastt:
                        split(4)
                        split(5)
                    accumulate(i, n + (3 if lastt else 4), st_, peeled and i == 0, lastt)

                pace.upto(base + AHEAD_F + 1)
                turn(0, True)
                with dve.Fori(1, NI - 1) as i:
                    turn(i, False)
                pace.n = base + 1 + 6 * (NI - 1) + AHEAD_F
                turn(NI - 1, True)

            pace = Pace(dve, split_lo, 0)
            dve.wait_ge(const_loaded, 16 * 11)
            pace.upto(AHEAD_F)
            for t in range(NT):
                xT_evac(t, t, xT_hi, xT_lo, T, t * P)
            ffn(0, 0)

            def rope(G, R, src, t, cs, half, heads, dst1, dst2):
                cos = cs[0:R, t * 2 * half:t * 2 * half + half]
                sin = cs[0:R, t * 2 * half + half:(t + 1) * 2 * half]
                n2 = 2 * heads
                a3 = tA[0:R, 0:n2 * half].rearrange("p (h c) -> p h c", c=half)
                b3 = tB[0:R, 0:n2 * half].rearrange("p (h c) -> p h c", c=half)
                s3 = src.rearrange("p (h c) -> p h c", c=half)
                tt(a3, s3, cos.unsqueeze(1).to_broadcast([R, n2, half]), ALU.mult)
                link(tt(b3, s3, sin.unsqueeze(1).to_broadcast([R, n2, half]), ALU.mult))
                return a3, b3

            n_unit = [0]
            for kind, G, x, n in TIMELINE:
                g = HR * G + x
                TGn = tokens_of(G)
                k = STAGE_PIECES.get(kind, 0)
                if k:
                    pace.stage(n, k)
                if kind == "XT":
                    xT_evac(NT + 3 * G + x, 3 * G + x, xg_hi, xg_lo, TG, x * P)
                    if x == 0 and G == 0:
                        dve.wait_ge(piece_used, MIX0)
                        nc.vector.memset(ka_prev[:], 0.0).then_inc(prev_zeroed, 1)
                        nc.vector.memset(va_prev[:], 0.0).then_inc(prev_zeroed, 1)
                elif kind == "P":
                    dve.wait_ge(piece_used, n + 4)
                    if x == 0:
                        dve.wait_ge(cs_loaded, 32 * (G + 1))
                    if g:
                        dve.wait_ge(tr_done, g)
                    for t in range(3):
                        R = rows_of(3 * G + t)
                        a3, b3 = rope(G, R, bank(t, R, 0, 2 * DK), t, cs_ret, DK // 2, 2, None, None)
                        av = a3.rearrange("p (q s) c -> p q s c", s=2)
                        bv = b3.rearrange("p (q s) c -> p q s c", s=2)
                        ov = qk[0:R, t * 2 * DK:(t + 1) * 2 * DK].rearrange("p (q s c) -> p q s c", s=2, c=DK // 2)
                        tt(ov[:, :, 0, :], av[:, :, 0, :], bv[:, :, 1, :], ALU.subtract)
                        ins = tt(ov[:, :, 1, :], av[:, :, 1, :], bv[:, :, 0, :], ALU.add)
                        if t < 2:
                            link(ins)
                    ins.then_inc(rope_read, 1)
                elif kind == "G":
                    dve.wait_ge(rope_read, g + 1)
                    if g:
                        dve.wait_ge(kv_done, kv_count(G, x - 1) if x else kv_count(G - 1, HR - 1))
                    for i, (t0, nt, R) in enumerate(parts_of(G)):
                        src = qk[0:R, :].rearrange("p (t c) -> p t c", t=3)[:, t0:t0 + nt, DK:]
                        dst = kdec[0:R, (g % 2) * 3 * DK:(g % 2 + 1) * 3 * DK].rearrange("p (t c) -> p t c", t=3)[:, t0:t0 + nt, :]
                        ins = nc.vector.tensor_scalar(dst, src, kdec_t[0:R, HR * i + x:HR * i + x + 1], None, ALU.mult)
                    ins.then_inc(kdec_ready, 1)
                elif kind == "TR" and G == NG - 1:
                    dve.wait_ge(qkT_ready, 2 * g + 1)
                    tt(qT_m[:].rearrange("p (b c) -> p b c", b=DB),
                       qT[:, 2 * P:2 * P + SR].unsqueeze(1).to_broadcast([P, DB, SR]),
                       batch_cols[:].rearrange("p (b c) -> p b c", b=DB), ALU.mult).then_inc(qTm_ready, 1)
                elif kind == "SKV":
                    dve.wait_ge(s_done, g + 1)
                    for i, (t0, nt, R) in enumerate(parts_of(G)):
                        src = ps[0:R, 6 * BANK + t0 * P:6 * BANK + (t0 + nt) * P].rearrange("p (t c) -> p t c", t=nt)[:, :, 0:R]
                        dst = pt_r[0:R, t0 * P:(t0 + nt) * P].rearrange("p (t c) -> p t c", t=nt)[:, :, 0:R]
                        msk = (ret_mask[:, x * P:(x + 1) * P] if i == 0 else ret_mask_s[0:SR, x * SR:(x + 1) * SR])
                        ins = tt(dst, src, msk.unsqueeze(1).to_broadcast([R, nt, R]), ALU.mult)
                    ins.then_inc(pt_ready, 1)
                    cd = CD_PROMPT[x]
                    src_slot, dst_slot = (x - G) % 5, (x - G - 1) % 5
                    chain_in = rst[:, src_slot * DV:(src_slot + 1) * DV]
                    ntp = 3 if G < NG - 1 else 2
                    base_kv = kv_count(G, x) - (2 if G < NG - 1 else 1)
                    for t in range(ntp):
                        dve.wait_ge(kv_done, base_kv + (1 if t < 2 else 2))
                        src = bank(7, P, t * DV, DV) if t < 2 else bank(6, P, 0, DV)
                        final = t == ntp - 1
                        dst = rst[:, dst_slot * DV:(dst_slot + 1) * DV] if final else r12[:, t * DV:(t + 1) * DV]
                        if G == 0 and t == 0:
                            ins = nc.vector.tensor_copy(dst, src)
                        else:
                            ins = nc.vector.scalar_tensor_tensor(out=dst, in0=chain_in, scalar=cd, in1=src,
                                                                 op0=ALU.mult, op1=ALU.add)
                        if final:
                            ins.then_inc(r_ready, 1)
                        else:
                            link(ins)
                        chain_in = dst
                elif kind == "PVQ":
                    dve.wait_ge(o_ready, g + 1)
                    for t in range(3):
                        R = rows_of(3 * G + t)
                        ins = nc.vector.bn_stats(gst[0:R, 6 * t:6 * t + 6], orow[0:R, t * DV:(t + 1) * DV])
                    link(ins)
                    for t in range(3):
                        R = rows_of(3 * G + t)
                        ins = nc.vector.bn_aggr(gmv[0:R, 2 * t:2 * t + 2], gst[0:R, 6 * t:6 * t + 6])
                    ins.then_inc(gn_aggr, 1)
                    dve.wait_ge(gn_rstd, g + 1)
                    for t in range(3):
                        R = rows_of(3 * G + t)
                        ot = orow[0:R, t * DV:(t + 1) * DV]
                        ins = nc.vector.tensor_scalar(ot, ot, gmv[0:R, 2 * t:2 * t + 1], grs[0:R, t:t + 1],
                                                      ALU.subtract, ALU.mult)
                    link(ins)
                    dve.wait_ge(gs_ready, g + 1)
                    for t0, nt, R in parts_of(G):
                        ot = orow[0:R, t0 * DV:(t0 + nt) * DV]
                        g0 = (g % 2) * 3 * DV
                        ins = tt(ot, ot, gs[0:R, g0 + t0 * DV:g0 + (t0 + nt) * DV], ALU.mult)
                    ins.then_inc(gn_done, 1)
                elif kind == "SU":
                    for half in range(2):
                        if x or half:
                            dve.wait_ge(su_done, 2 * x + half)
                        tt(kdec_m[0:SR, :].rearrange("p (b c) -> p b c", b=4),
                           kdec[0:SR, (3 * (g % 2) + 2) * DK:(3 * (g % 2) + 3) * DK].unsqueeze(1).to_broadcast([SR, 4, DK]),
                           batch_rows[0:SR, 4 * half:4 * half + 4].unsqueeze(2).to_broadcast([SR, 4, DK]),
                           ALU.mult).then_inc(kdm_ready, 1)
                        dve.wait_ge(su_done, 2 * x + half + 1)
                        sl = st[:, half * 4 * DV:(half + 1) * 4 * DV]
                        nc.vector.scalar_tensor_tensor(out=sl, in0=sl, scalar=CD_SAMPLE[x], in1=ps[:, 6 * BANK:8 * BANK],
                                                       op0=ALU.mult, op1=ALU.add).then_inc(st_ready, 1)
                elif kind == "T":
                    dve.wait_ge(or_hi_ready, g + 1)
                    src = ps[:, 6 * BANK:8 * BANK].rearrange("p (e c) -> p e c", e=2)[:, :, 0:TGn]
                    hi = fr(orT_hi[:].rearrange("p (e c) -> p e c", e=2)[:, :, 0:TGn])
                    lo = orT_lo[:].rearrange("p (e c) -> p e c", e=2)[:, :, 0:TGn]
                    tt(lo, src, hi, ALU.subtract).then_inc(or_lo_ready, 1)
                elif kind == "B":
                    for f in range(KT):
                        if f < KT - 1:
                            dve.wait_ge(b_done, 7 * g + f + 1)
                        else:
                            dve.wait_ge(piece_used, n + 2)
                        dst = racc[:, f * TG:f * TG + TGn]
                        if x == 0:
                            ins = nc.vector.tensor_copy(dst, bank(6 + f % 2, n=TGn))
                        else:
                            ins = tt(dst, dst, bank(6 + f % 2, n=TGn), ALU.add)
                        ins.then_inc(racc_done, 1)
                elif kind == "MB":
                    dve.wait_ge(racc_done, 8 * HR * (G + 1))
                    for f in range(KT):
                        dve.wait_ge(sig_done, 16 * G + f + 1)
                        rf = racc[:, f * TG:f * TG + TGn]
                        tt(rf, rf, sig[:, f * TG:f * TG + TGn], ALU.mult).then_inc(mb_done, 1)
                elif kind == "KVA":
                    dve.wait_ge(piece_used, n + 2)
                    for t in range(3):
                        R = rows_of(3 * G + t)
                        a3, b3 = rope(G, R, bank(3 + t, R, 0, P), t, cs_att, HD // 2, HKV, None, None)
                        av = a3.rearrange("p (q s) c -> p q s c", s=2)
                        bv = b3.rearrange("p (q s) c -> p q s c", s=2)
                        ov = ka[0:R, t * P:(t + 1) * P].rearrange("p (q s c) -> p q s c", s=2, c=HD // 2)
                        tt(ov[:, :, 0, :], av[:, :, 0, :], bv[:, :, 1, :], ALU.subtract)
                        ins = tt(ov[:, :, 1, :], av[:, :, 1, :], bv[:, :, 0, :], ALU.add)
                        if t < 2:
                            link(ins)
                    ins.then_inc(ka_ready, 1)
                    dve.wait_ge(ka_ready, G + 1)
                elif kind == "TRQ":
                    t = x
                    R = rows_of(3 * G + t)
                    if t == 2:
                        dve.wait_ge(trq_done, 3 * G + 1)
                    a3, b3 = rope(G, R, bank(t, R), t, cs_att, HD // 2, HQ, None, None)
                    ob = qa[0:R, (t % 2) * 512:(t % 2 + 1) * 512].rearrange("p (g n s c) -> p n g s c", g=GQ, n=HKV, s=2)
                    av = a3.rearrange("p (n g s) c -> p n g s c", n=HKV, s=2)
                    bv = b3.rearrange("p (n g s) c -> p n g s c", n=HKV, s=2)
                    tt(ob[:, :, :, 0, :], av[:, :, :, 0, :], bv[:, :, :, 1, :], ALU.subtract)
                    tt(ob[:, :, :, 1, :], av[:, :, :, 1, :], bv[:, :, :, 0, :], ALU.add).then_inc(qa_ready, 1)
                    dve.wait_ge(qa_ready, 3 * G + t + 1)
                elif kind in ("AS", "SS"):
                    u = n_unit[0]
                    n_unit[0] += 1
                    wd = 2 * WIN if kind == "AS" else 192
                    pb = prob[:, (u % 2) * 1024:(u % 2) * 1024 + 4 * wd]
                    p3 = pb.rearrange("p (q c) -> p q c", q=4)
                    dve.wait_ge(as_done, u + 1)
                    if u >= 2:
                        dve.wait_ge(ap_done, u - 1)
                    if kind == "AS":
                        t, nkv = units_of(G)[x]
                        msk = att_mask[:, 256:512] if (G or t) else att_mask[:, 0:256]
                        ins = nc.vector.scalar_tensor_tensor(
                            out=p3, in0=ps[:, 3 * BANK:5 * BANK].rearrange("p (q c) -> p q c", q=4), scalar=HD ** -0.5,
                            in1=msk.unsqueeze(1).to_broadcast([P, 4, 256]), op0=ALU.mult, op1=ALU.add)
                        snk = sinks[:, nkv * 4:nkv * 4 + 4]
                    else:
                        for nkv in range(HKV):
                            ins = nc.vector.scalar_tensor_tensor(
                                out=pb[:, nkv * 384:(nkv + 1) * 384], in0=bank(3 + nkv, n=384), scalar=HD ** -0.5,
                                in1=att_mask_s[:], op0=ALU.mult, op1=ALU.add)
                    ins.then_inc(sm_read, 1)
                    dve.wait_ge(sm_read, u + 1)
                    link(nc.vector.tensor_reduce(mx[:, 0:4], p3, AXX, ALU.max))
                    if kind == "AS":
                        link(tt(mx[:, 0:4], mx[:, 0:4], snk, ALU.max))
                        tt(esd[:, 0:4], snk, mx[:, 0:4], ALU.subtract)
                    else:
                        s2 = sinks_s[:, :].unsqueeze(2).to_broadcast([P, 2, 2])
                        m2 = mx[:, 0:4].rearrange("p (n b) -> p n b", b=2)
                        link(tt(m2, m2, s2, ALU.max))
                        tt(esd[:, 0:4].rearrange("p (n b) -> p n b", b=2), s2, m2, ALU.subtract)
                    nc.vector.tensor_scalar(nmx[:, 0:4], mx[:, 0:4], -1.0, None, ALU.mult).then_inc(nmx_ready, 1)
                    dve.wait_ge(exp_done, u + 1)
                    link(tt(den[:, 0:4], rsum[:, 0:4], es[:, 0:4], ALU.add))
                    link(nc.vector.reciprocal(rden[:, 0:4], den[:, 0:4]))
                    tt(p3, p3, rden[:, 0:4].unsqueeze(2).to_broadcast([P, 4, wd]), ALU.mult).then_inc(p_ready, 1)
                elif (kind == "AV" and x % 2 == 1) or kind == "SV":
                    t = x // 2 if kind == "AV" else 2
                    R = rows_of(3 * G + t)
                    dve.wait_ge(oa_hi_ready, 3 * G + t + 1)
                    hi = fr(oaT_hi[:].rearrange("p (k c) -> p k c", k=4)[:, :, t * P:t * P + R])
                    lo = oaT_lo[:].rearrange("p (k c) -> p k c", k=4)[:, :, t * P:t * P + R]
                    tt(lo, bank(2).rearrange("p (k c) -> p k c", k=4)[:, :, 0:R], hi, ALU.subtract).then_inc(oa_lo_ready, 1)
                elif kind == "A":
                    dve.wait_ge(piece_used, n + 1)
                    dve.wait_ge(sig_done, 16 * (G + 1))
                    b0 = 0 if x % 2 == 0 else 3
                    for f2 in range(2):
                        sf = sig[:, (2 * x + f2) * TG:(2 * x + f2) * TG + TGn]
                        ins = tt(sf, sf, bank(b0 + f2, n=TGn), ALU.mult)
                    link(ins)
                    for f2 in range(2):
                        f = 2 * x + f2
                        sf = sig[:, f * TG:f * TG + TGn]
                        tt(sf, sf, racc[:, f * TG:f * TG + TGn], ALU.add).then_inc(m_ready, 1)
                    dve.wait_ge(m_hi_ready, 4 * G + x + 1)
                    src = sig[:, 2 * x * TG:(2 * x + 2) * TG].rearrange("p (f c) -> p f c", f=2)[:, :, 0:TGn]
                    b = (x % 2) * 2 * TG
                    hi = fr(mT_hi[:, b:b + 2 * TG].rearrange("p (f c) -> p f c", f=2)[:, :, 0:TGn])
                    lo = mT_lo[:, b:b + 2 * TG].rearrange("p (f c) -> p f c", f=2)[:, :, 0:TGn]
                    tt(lo, src, hi, ALU.subtract).then_inc(m_lo_ready, 1)
                elif kind == "WO":
                    for q in range(6):
                        t = 3 * G + q // 2
                        R = rows_of(t)
                        if x == 0 and q % 2 == 0:
                            dve.wait_ge(y_scaled, NT + t + 1)
                        if q < 5:
                            dve.wait_ge(wo_done, 5 * (4 * G + x) + q + 1)
                        else:
                            dve.wait_ge(piece_used, n + 2)
                        ysl = y[0:R, t * D + (q % 2) * 512:t * D + (q % 2) * 512 + 512]
                        tt(ysl, ysl, bank([2, 5, 6, 7][q % 4], R), ALU.add).then_inc(wacc_done, 1)
                elif kind == "LN":
                    dve.wait_ge(wacc_done, 24 * (G + 1))
                    ln_stats(3 * G + x)

            dve.wait_ge(st_stored, 16 * HR)
            dve.wait_ge(out_stored, 16 * (2 + HR + 2 + 2 * DB))
            for t in range(NT):
                xT_evac(2 * NT + t, t, xT_hi, xT_lo, T, t * P)
            ffn(1, FFN2_0)

        @block.tensor
        def _(pe):
            mm = nc.tensor.matmul

            def three(out, a_hi, a_lo, b_hi, b_lo, first, last):
                mm(out, a_hi, b_hi, start=first, stop=False)
                mm(out, a_hi, b_lo, start=False, stop=False)
                return mm(out, a_lo, b_hi, start=False, stop=last)

            def xT_pe(v, t):
                R = rows_of(t)
                if v >= 2:
                    pe.wait_ge(xT_lo_ready, v - 1)
                base = (3 if v % 2 else 0) * BANK
                for k in range(KT):
                    ins = nc.tensor.transpose(ps[:, base + k * P:base + k * P + R], y[0:R, t * D + k * P:t * D + (k + 1) * P],
                                              ident[0:R, 0:R])
                ins.then_inc(xt_done, 1)

            def up(b0, n):
                wh, wl = wslot(n, False), wslot(n, True)
                for k in range(KT):
                    for ci, (c0, cw) in enumerate(CHUNKS):
                        out = bank(b0 + ci, n=cw)
                        xh, xl = xT_hi[:, k * T + c0:k * T + c0 + cw], xT_lo[:, k * T + c0:k * T + c0 + cw]
                        mm(out, wh[:, k * P:(k + 1) * P], xh, start=(k == 0), stop=False)
                        mm(out, wh[:, k * P:(k + 1) * P], xl, start=False, stop=False)
                    for ci, (c0, cw) in enumerate(CHUNKS):
                        ins = mm(bank(b0 + ci, n=cw), wl[:, k * P:(k + 1) * P], xT_hi[:, k * T + c0:k * T + c0 + cw],
                                 start=False, stop=(k == KT - 1))
                ins.then_inc(piece_used, 1)

            def ffn(f, base):
                J0, I0 = NJ * f, NI * f

                def turn(i, peeled):
                    st_ = 0 if peeled else 6
                    n = base + 1 + (6 * i if peeled else 0)
                    J = i * 2 + J0
                    lastt = peeled and i == NI - 1
                    pe.wait_ge(lo_ready, n + 1 + st_ * i)
                    up(3, n)
                    pe.wait_ge(lo_ready, n + 2 + st_ * i)
                    pe.wait_ge(silu_done, J * 3 + 3)
                    up(0, n + 1)
                    pe.wait_ge(lo_ready, n + 3 + st_ * i)
                    pe.wait_ge(h_mul, J * 3 + 3)
                    up(3, n + 2)
                    if not lastt:
                        pe.wait_ge(lo_ready, n + 4 + st_ * i)
                        pe.wait_ge(silu_done, J * 3 + 6)
                        up(0, n + 3)
                    nw = n + (3 if lastt else 4)
                    pe.wait_ge(lo_ready, nw + 2 + st_ * i)
                    pe.wait_ge(h_lo_ready, J * 3 + 6)
                    if not (peeled and i == 0 and f == 0):
                        pe.wait_ge(acc_done, (i + I0) * 18)
                    for q in range(2 * NT):
                        t, half = q // 2, q % 2
                        R = rows_of(t)
                        if q >= 5:
                            pe.wait_ge(acc_done, (i + I0) * 18 + q - 4)
                        out = bank(DOWN_BANKS[q % 5], R)
                        for s in range(2):
                            a = s * T + t * P
                            ins = three(out, h_hi[:, a:a + R], h_lo[:, a:a + R],
                                        wslot(nw + s, False)[:, half * 512:(half + 1) * 512],
                                        wslot(nw + s, True)[:, half * 512:(half + 1) * 512], s == 0, s == 1)
                        if q < 2 * NT - 1:
                            ins.then_inc(down_done, 1)
                    ins.then_inc(piece_used, 2)
                    pe.wait_ge(acc_done, (i + I0) * 18 + 16)

                pe.wait_ge(xT_lo_ready, 2 * NT * f + NT)
                pe.wait_ge(lo_ready, base + 1)
                up(0, base)
                turn(0, True)
                with pe.Fori(1, NI - 1) as i:
                    turn(i, False)
                turn(NI - 1, True)

            pe.wait_ge(const_loaded, 16 * 11)
            for t in range(NT):
                pe.wait_ge(x_loaded[t], 16)
                xT_pe(t, t)
            ffn(0, 0)

            def misc_free(G, kind, x):
                cnt = {}
                for kk, gg, xx, nn in TIMELINE:
                    if (kk, gg, xx) == (kind, G, x):
                        break
                    if kk in MISC_READERS:
                        cnt[kk] = cnt.get(kk, 0) + 1
                for kk, v in cnt.items():
                    s, per = MISC_READERS[kk]
                    pe.wait_ge(s, per * v)

            MISC_READERS = {"TR": (qkT_ready, 2), "SKV": (r_ready, 1), "PVQ": (o_ready, 1), "T": (or_lo_ready, 1),
                            "B": (racc_done, 8), "SU": (st_ready, 2), "TRK": (kaT_ready, 1), "KC": (kcT_ready, 1)}

            def token_major(n, npieces, kper, width, b0, G):
                for i in range(npieces):
                    pe.wait_ge(lo_ready, n + i + 1)
                    wh, wl = wslot(n + i, False), wslot(n + i, True)
                    for kk in range(kper):
                        k = i * kper + kk
                        for t in range(3):
                            R = rows_of(3 * G + t)
                            a = k * TG + t * P
                            ins = three(bank(b0 + t, R, 0, width), xg_hi[:, a:a + R], xg_lo[:, a:a + R],
                                        wh[:, kk * width:(kk + 1) * width], wl[:, kk * width:(kk + 1) * width],
                                        k == 0, k == KT - 1)
                    ins.then_inc(piece_used, 1)

            def gate(n, b, G):
                TGn = tokens_of(G)
                pe.wait_ge(lo_ready, n + 1)
                wh, wl = wslot(n, False), wslot(n, True)
                for k in range(KT):
                    ins = three(bank(b, n=TGn), wh[:, k * P:(k + 1) * P], wl[:, k * P:(k + 1) * P],
                                xg_hi[:, k * TG:k * TG + TGn], xg_lo[:, k * TG:k * TG + TGn], k == 0, k == KT - 1)
                ins.then_inc(piece_used, 1)

            for kind, G, x, n in TIMELINE:
                g = HR * G + x
                TGn = tokens_of(G)
                last_group = G == NG - 1
                if kind == "XT":
                    pe.wait_ge(ln_affine, 3 * G + x + 1)
                    if G == 0 and x == 0:
                        pe.wait_ge(acc_done, 18 * NI)
                    xT_pe(NT + 3 * G + x, 3 * G + x)
                elif kind == "P":
                    if x == 0:
                        pe.wait_ge(xT_lo_ready, NT + 3 * G + 3)
                    if g:
                        pe.wait_ge(rope_read, g)
                        pe.wait_ge(v_ready, g)
                    token_major(n, 4, 2, 512, 0, G)
                elif kind == "G":
                    if g:
                        pe.wait_ge(gs_ready, g)
                    token_major(n, 2, 4, DV, 3, G)
                elif kind == "TR":
                    pe.wait_ge(rope_read, g + 1)
                    misc_free(G, kind, x)
                    for s in range(2):
                        for t in range(3):
                            R = rows_of(3 * G + t)
                            ins = nc.tensor.transpose(bank(6 + s, P, t * P, R),
                                                      qk[0:R, t * 2 * DK + s * DK:t * 2 * DK + (s + 1) * DK], ident[0:R, 0:R])
                    ins.then_inc(tr_done, 1)
                elif kind == "SKV":
                    pe.wait_ge(qkT_ready, 2 * g + 2)
                    misc_free(G, kind, x)
                    for t in range(3):
                        R = rows_of(3 * G + t)
                        ins = mm(bank(6, R, t * P, R), kT[:, t * P:t * P + R], qT[:, t * P:t * P + R], start=True, stop=True)
                    ins.then_inc(s_done, 1)
                    pe.wait_ge(kdec_ready, g + 1)
                    pe.wait_ge(v_ready, g + 1)
                    vb, kb = (g % 2) * 3 * DV, (g % 2) * 3 * DK
                    for t in range(2):
                        ins = mm(bank(7, P, t * DV, DV), kdec[:, kb + t * DK:kb + (t + 1) * DK], v_r[:, vb + t * DV:vb + (t + 1) * DV],
                                 start=True, stop=True)
                    ins.then_inc(kv_done, 1)
                    if not last_group:
                        pe.wait_ge(pt_ready, g + 1)
                        mm(bank(6, P, 0, DV), kdec[:, kb + 2 * DK:kb + 3 * DK], v_r[:, vb + 2 * DV:vb + 3 * DV],
                           start=True, stop=True).then_inc(kv_done, 1)
                elif kind == "PVQ":
                    pe.wait_ge(pt_ready, g + 1)
                    pe.wait_ge(r_ready, g + 1)
                    misc_free(G, kind, x)
                    vb = (g % 2) * 3 * DV
                    slot = (x - G) % 5
                    for t in range(3):
                        R = rows_of(3 * G + t)
                        sample = last_group and t == 2
                        out = ps[0:R, 6 * BANK + t * DV:6 * BANK + (t + 1) * DV]
                        no_state = G == 0 and t == 0
                        ins = mm(out, pt_r[0:R, t * P:t * P + R], v_r[0:R, vb + t * DV:vb + (t + 1) * DV],
                                 start=True, stop=no_state)
                        if sample:
                            pe.wait_ge(qTm_ready, x + 1)
                            pe.wait_ge(st_loaded, 16 * (x + 1))
                            for b in range(DB):
                                ins = mm(out, qT_m[:, b * SR:(b + 1) * SR], st[:, b * DV:(b + 1) * DV], start=False, stop=(b == DB - 1))
                        elif not no_state:
                            state = rst[:, slot * DV:(slot + 1) * DV] if t == 0 else r12[:, (t - 1) * DV:t * DV]
                            ins = mm(out, qT[:, t * P:t * P + R], state, start=False, stop=True)
                    ins.then_inc(pvq_done, 1)
                elif kind == "SU":
                    vb = (g % 2) * 3 * DV
                    for half in range(2):
                        if half == 0:
                            misc_free(G, kind, x)
                        else:
                            pe.wait_ge(st_ready, 2 * x + 1)
                        pe.wait_ge(kdm_ready, 2 * x + half + 1)
                        for b in range(4):
                            ins = mm(ps[:, 6 * BANK + b * DV:6 * BANK + (b + 1) * DV], kdec_m[0:SR, b * DK:(b + 1) * DK],
                                     v_r[0:SR, vb + 2 * DV:vb + 3 * DV], start=True, stop=True)
                        ins.then_inc(su_done, 1)
                elif kind == "T":
                    pe.wait_ge(gn_done, g + 1)
                    misc_free(G, kind, x)
                    for e in range(2):
                        for t in range(3):
                            R = rows_of(3 * G + t)
                            ins = nc.tensor.transpose(bank(6 + e, P, t * P, R), orow[0:R, t * DV + e * P:t * DV + (e + 1) * P],
                                                      ident[0:R, 0:R])
                    ins.then_inc(t_done, 1)
                elif kind == "B":
                    pe.wait_ge(lo_ready, n + 2)
                    pe.wait_ge(or_lo_ready, g + 1)
                    misc_free(G, kind, x)
                    for f in range(KT):
                        if f >= 2:
                            pe.wait_ge(racc_done, 8 * g + f - 1)
                        for e in range(2):
                            fs = slice(f * P, (f + 1) * P)
                            ins = three(bank(6 + f % 2, n=TGn), wslot(n + e, False)[:, fs], wslot(n + e, True)[:, fs],
                                        orT_hi[:, e * TG:e * TG + TGn], orT_lo[:, e * TG:e * TG + TGn], e == 0, e == 1)
                        if f < KT - 1:
                            ins.then_inc(b_done, 1)
                    ins.then_inc(piece_used, 2)
                elif kind == "GB":
                    if x == 0:
                        pe.wait_ge(rope_read, HR * (G + 1))
                        pe.wait_ge(v_ready, HR * (G + 1))
                    if x >= 3:
                        pe.wait_ge(sig_done, 16 * G + x - 2)
                    gate(n, x % 3, G)
                elif kind == "GA":
                    if x == 0:
                        misc_free(G, kind, x)
                    if x >= 2:
                        pe.wait_ge(sig_done, 16 * G + 8 + x - 1)
                    gate(n, 6 + x % 2, G)
                elif kind == "QA":
                    pe.wait_ge(sig_done, 16 * G + 8)
                    token_major(n, 4, 2, 512, 0, G)
                elif kind == "KVA":
                    pe.wait_ge(gs_ready, HR * (G + 1))
                    token_major(n, 2, 4, 256, 3, G)
                elif kind == "TRK":
                    pe.wait_ge(ka_ready, G + 1)
                    pe.wait_ge(va_ready, G + 1)
                    misc_free(G, kind, x)
                    for t in range(3):
                        R = rows_of(3 * G + t)
                        ins = nc.tensor.transpose(bank(7, P, t * P, R), ka[0:R, t * P:(t + 1) * P], ident[0:R, 0:R])
                    ins.then_inc(trk_done, 1)
                elif kind == "TRQ":
                    R = rows_of(3 * G + x)
                    pe.wait_ge(qa_ready, 3 * G + x + 1)
                    if x:
                        pe.wait_ge(qaT_ready, 3 * G + x)
                    for q in range(GQ):
                        ins = nc.tensor.transpose(bank(5, P, q * P, R), qa[0:R, (x % 2) * 512 + q * P:(x % 2) * 512 + (q + 1) * P],
                                                  ident[0:R, 0:R])
                    ins.then_inc(trq_done, 1)
                elif kind == "KC":
                    pe.wait_ge(kc_loaded, 16)
                    misc_free(G, kind, x)
                    for b in range(DB):
                        ins = nc.tensor.transpose(ps[:, 6 * BANK + b * P:6 * BANK + (b + 1) * P], prob[:, b * P:(b + 1) * P], ident[:])
                    ins.then_inc(kc_tr, 1)
                elif kind == "AS":
                    t, nkv = units_of(G)[x]
                    u = len(units_of(0)) * G + x
                    pe.wait_ge(kaT_ready, G + 1)
                    pe.wait_ge(qaT_ready, 3 * G + 3)
                    if u:
                        pe.wait_ge(sm_read, u)
                    pr = slice(nkv * HD, (nkv + 1) * HD)
                    for q in range(GQ):
                        ins = mm(ps[:, 3 * BANK + q * 256:3 * BANK + (q + 1) * 256],
                                 qaT[pr, t * 512 + q * P:t * 512 + (q + 1) * P], kaT[pr, t * P:(t + 2) * P], start=True, stop=True)
                    ins.then_inc(as_done, 1)
                elif kind == "AP":
                    u = len(units_of(0)) * G + x
                    pe.wait_ge(p_ready, u + 1)
                    if u:
                        pe.wait_ge(pT_ready, u)
                    pb = (u % 2) * 1024
                    for q in range(8):
                        ins = nc.tensor.transpose(ps[:, q * P:(q + 1) * P], prob[:, pb + q * P:pb + (q + 1) * P], ident[:])
                    ins.then_inc(ap_done, 1)
                elif kind == "AV":
                    t, nkv = units_of(G)[x]
                    u = len(units_of(0)) * G + x
                    pe.wait_ge(pT_ready, u + 1)
                    if nkv == 0 and 3 * G + t:
                        pe.wait_ge(oa_lo_ready, 3 * G + t)
                    for q in range(GQ):
                        r0 = (q % 2) * HD
                        out = ps[r0:r0 + HD, 2 * BANK + (2 * nkv + q // 2) * P:2 * BANK + (2 * nkv + q // 2 + 1) * P]
                        for s in range(2):
                            ins = mm(out, va[:, (t + s) * P + nkv * HD:(t + s) * P + (nkv + 1) * HD],
                                     probT[:, (2 * q + s) * P:(2 * q + s + 1) * P], start=(s == 0), stop=(s == 1))
                    ins.then_inc(av_done, 1)
                elif kind == "SS":
                    u = len(units_of(0)) * G + 4
                    pe.wait_ge(kcT_ready, 1)
                    pe.wait_ge(sm_read, u)
                    for bh in range(2):
                        for nkv in range(HKV):
                            pr = slice(nkv * HD, (nkv + 1) * HD)
                            for b4 in range(4):
                                b = bh * 4 + b4
                                lhs = qaT[pr, 2 * 512 + b * GQ * DT:2 * 512 + (b + 1) * GQ * DT]
                                o0 = (3 + nkv) * BANK + bh * 192
                                mm(ps[32 * b4:32 * b4 + 32, o0:o0 + P], lhs, kcT[pr, b * P:(b + 1) * P], start=True, stop=True)
                                ins = mm(ps[32 * b4:32 * b4 + 32, o0 + P:o0 + P + SR], lhs, kaT[pr, 3 * P:3 * P + SR],
                                         start=True, stop=True)
                    ins.then_inc(as_done, 1)
                elif kind == "SP":
                    u = len(units_of(0)) * G + 4
                    pe.wait_ge(p_ready, u + 1)
                    pe.wait_ge(pT_ready, u)
                    pb = (u % 2) * 1024
                    for q in range(4):
                        nc.tensor.transpose(bank(0, P, q * P, P), prob[:, pb + q * 192:pb + q * 192 + P], ident[:])
                    for q in range(4):
                        ins = nc.tensor.transpose(bank(1, SR, q * P, P), prob[:, pb + q * 192 + P:pb + (q + 1) * 192], ident[:])
                    ins.then_inc(ap_done, 1)
                elif kind == "SV":
                    u = len(units_of(0)) * G + 4
                    pe.wait_ge(pT_ready, u + 1)
                    pe.wait_ge(oa_lo_ready, 3 * G + 2)
                    pe.wait_ge(vc_loaded, 16)
                    for b in range(DB):
                        for nkv in range(HKV):
                            for par in range(2):
                                o3 = ps[par * HD:(par + 1) * HD, 2 * BANK + 2 * nkv * P:2 * BANK + (2 * nkv + 2) * P]\
                                    .rearrange("p (k c) -> p k c", k=2)[:, :, b * DT:(b + 1) * DT]
                                q = nkv * 2 + b // 4

                                def cols(base, rws):
                                    c0 = base + q * P + (b % 4) * 32
                                    return probT[0:rws, c0:c0 + 32].rearrange("p (h s t) -> p h s t", h=2, s=2)[:, :, par, :]
                                mm(o3, vc[:, b * P + nkv * HD:b * P + (nkv + 1) * HD], cols(0, P), start=True, stop=False)
                                ins = mm(o3, va[0:SR, 3 * P + nkv * HD:3 * P + (nkv + 1) * HD], cols(512, SR),
                                         start=False, stop=True)
                    ins.then_inc(av_done, 1)
                elif kind == "A":
                    pe.wait_ge(lo_ready, n + 1)
                    if x == 0:
                        pe.wait_ge(oa_lo_ready, 3 * G + 3)
                        pe.wait_ge(pT_ready, 6 * G + (6 if not last_group else 5))
                    if x == 2:
                        pe.wait_ge(m_ready, KT * G + 2)
                    if x == 3:
                        pe.wait_ge(m_ready, KT * G + 4)
                    b0 = 0 if x % 2 == 0 else 3
                    for f2 in range(2):
                        for k in range(4):
                            cs = slice(k * 256 + f2 * P, k * 256 + (f2 + 1) * P)
                            ins = three(bank(b0 + f2, n=TGn), wslot(n, False)[:, cs], wslot(n, True)[:, cs],
                                        oaT_hi[:, k * TG:k * TG + TGn], oaT_lo[:, k * TG:k * TG + TGn], k == 0, k == 3)
                    ins.then_inc(piece_used, 1)
                elif kind == "WO":
                    pe.wait_ge(lo_ready, n + 2)
                    pe.wait_ge(m_lo_ready, 4 * G + x + 1)
                    if x == 0:
                        pe.wait_ge(sig_done, 16 * (G + 1))
                    mb = (x % 2) * 2 * TG
                    for q in range(6):
                        t, half = q // 2, q % 2
                        R = rows_of(3 * G + t)
                        k = 24 * G + 6 * x + q
                        if q >= 4 or x:
                            pe.wait_ge(wacc_done, k - 3 if q >= 4 else 24 * G + 6 * x)
                        for f2 in range(2):
                            a = mb + f2 * TG + t * P
                            ins = three(bank([2, 5, 6, 7][q % 4], R), mT_hi[:, a:a + R], mT_lo[:, a:a + R],
                                        wslot(n + f2, False)[:, half * 512:(half + 1) * 512],
                                        wslot(n + f2, True)[:, half * 512:(half + 1) * 512], f2 == 0, f2 == 1)
                        if q < 5:
                            ins.then_inc(wo_done, 1)
                    ins.then_inc(piece_used, 2)

            for t in range(NT):
                pe.wait_ge(ln_affine, NT + t + 1)
                xT_pe(2 * NT + t, t)
            ffn(1, FFN2_0)


def kv_count(G, x):
    return 2 * (HR * G + x + 1) if G < NG - 1 else 2 * HR * (NG - 1) + x + 1


def shape_constants():
    f4 = np.float32
    c = {"ident": np.eye(P, dtype=f4)}
    inv_att = f4(1.0) / np.power(f4(10000.0), np.arange(0, HD, 2, dtype=f4) / f4(HD)).astype(f4)
    inv_ret = f4(1.0) / np.power(f4(10000.0), np.linspace(0.0, 1.0, DK // 2, dtype=f4)).astype(f4)
    pos = np.zeros((NT, P), dtype=f4)
    pos[:NT - 1] = np.arange(SEQ, dtype=f4).reshape(NT - 1, P)
    pos[NT - 1, :SR] = PAST + np.arange(SR) % DT
    for name, inv in (("cs_att", inv_att), ("cs_ret", inv_ret)):
        ang = (pos[:, :, None] * inv[None, None, :]).astype(f4).astype(np.float64)
        cs = np.stack([np.cos(ang), np.sin(ang)], axis=2).astype(f4)
        c[name] = np.ascontiguousarray(cs.reshape(NG, 3, P, -1).transpose(2, 0, 1, 3).reshape(P, NG, -1))
    i = np.arange(P)
    scale = DK ** -0.5
    c["ret_mask"] = np.stack([(i[:, None] <= i[None, :]) * np.exp(-(i[:, None] + 1) * g) * scale for g in LOG_G], 1)\
        .reshape(P, HR * P).astype(f4)
    r = np.arange(SR)
    b, t = r // DT, r % DT
    same = (b[:, None] == b[None, :]) & (t[:, None] <= t[None, :])
    c["ret_mask_s"] = np.stack([same * np.exp(-(t[:, None] + 1) * g) * scale for g in LOG_G], 1).reshape(SR, HR * SR).astype(f4)
    kd, qd = np.zeros((P, 2 * HR)), np.zeros((P, 2 * HR))
    for h, g in enumerate(LOG_G):
        kd[:, h], qd[:, h] = np.exp((P - 1 - i) * g) * scale, np.exp((i + 1) * g)
        kd[:, HR + h], qd[:, HR + h] = np.exp((DT - 1 - i % DT) * g) * scale, np.exp((i % DT + 1) * g)
    c["kdec_t"], c["qdec_t"] = kd.astype(f4), qd.astype(f4)
    own = np.where(i[None, :] <= i[:, None], 0.0, NEG)
    prev = np.where(i[None, :] > i[:, None], 0.0, NEG)
    none = np.full((P, P), NEG)
    c["att_mask"] = np.concatenate([none, own, prev, own], 1).astype(f4)
    row_b, row_t = i // 32, i % DT
    ms = np.full((P, 2, 192), NEG)
    for bh in range(2):
        ms[:, bh, :P] = np.where(i[None, :] > row_t[:, None], 0.0, NEG)
        ms[:, bh, P:] = np.where((b[None, :] == (bh * 4 + row_b)[:, None]) & (t[None, :] <= row_t[:, None]), 0.0, NEG)
    c["att_mask_s"] = ms.reshape(P, 384).astype(f4)
    onehot = (b[None, :] == np.arange(DB)[:, None]).astype(f4)
    c["batch_cols"] = np.ascontiguousarray(np.broadcast_to(onehot.reshape(1, -1), (P, DB * SR)))
    c["batch_rows"] = np.ascontiguousarray(onehot.T)
    return c


_INS = ["x_prompt", "x_sample", "cache_k", "cache_v", "state_ret", "ln_g", "ln_b", "ffn_wi", "ffn_wo", "w_in",
        "w_br_attn", "w_br_ret", "w_o"]
_OUTS = [("y_prompt", (1, SEQ, D)), ("y_sample", (DB, DT, D)), ("kcp", (1, 1, WIN, HKV, HD)), ("vcp", (1, 1, WIN, HKV, HD)),
         ("rp", (1, 1, HR, DK, DV)), ("kcs", (1, DB, WIN, HKV, HD)), ("vcs", (1, DB, WIN, HKV, HD)),
         ("rs", (1, DB, HR, DK, DV))]


def kernel(**inputs):
    import concourse.bacc as _bacc
    from concourse.bass_utils import run_bass_kernel_spmd as _run

    nc = _bacc.Bacc("TRN2", target_bir_lowering=False, num_devices=1)
    arrays, w, c, o = {}, {}, {}, {}
    for name in _INS:
        a = np.ascontiguousarray(inputs[name])
        arrays[f"in_{name}"] = a
        w[name] = nc.dram_tensor(f"in_{name}", a.shape, F32, kind="ExternalInput").ap()
    for name in ("w_in", "w_br_attn", "w_br_ret", "w_o"):
        w[name] = w[name][0]
    consts = shape_constants()
    sk = np.asarray(inputs["attn_sinks"])[0]
    consts["sinks"] = np.ascontiguousarray(np.broadcast_to(sk[None, :], (P, HQ)))
    consts["sinks_s"] = np.ascontiguousarray(np.tile(np.repeat(sk.reshape(HKV, GQ).T, DT, axis=0), (4, 1)))
    for name, a in consts.items():
        arrays[f"c_{name}"] = a
        c[name] = nc.dram_tensor(f"c_{name}", a.shape, F32, kind="ExternalInput").ap()
    for name, shape in _OUTS:
        o[name] = nc.dram_tensor(f"out_{name}", shape, F32, kind="ExternalOutput").ap()
    hybrid_layer(nc, w, c, o)
    r = _run(nc, [arrays], core_ids=[0])
    return tuple(r.results[0][f"out_{name}"] for name, _ in _OUTS)
```

```python
from contextlib import ExitStack

import numpy as np

import concourse.bass as bass
from concourse import mybir

F32 = mybir.dt.float32
FR = mybir.dt.float32r
ACT = mybir.ActivationFunctionType
ALU = mybir.AluOpType
AXX = mybir.AxisListType.X

P = 128
D = 1024
KT = D // P
DFF = 2816
NJ = DFF // P
NI = NJ // 2
SEQ, DB, DT = 1024, 8, 8
PAST = 4096
T = SEQ + DB * DT
NT = (T + P - 1) // P
SR = DB * DT
BANK = 512
HQ, HKV, HD = 8, 2, 64
GQ = HQ // HKV
HR, DK, DV = 4, 128, 256
WIN = 128
NG = 3
TG = 3 * P
ALPHA = 2.0 ** 0.25
LN_EPS, GN_EPS = 1e-5, 1e-6
NEG = -1e30
RAW = 3
FSLOTS, MSLOTS = 6, 4
AHEAD_F, AHEAD_M = 4, 3
NP_PHASE = 66
MIX0 = NP_PHASE
FFN2_0 = MIX0 + NG * NP_PHASE
NPIECES = FFN2_0 + NP_PHASE
OFF = {}
_o = 0
for _n, _w in (("qa", 512), ("ka", 128), ("va", 128), ("qr", 512), ("kr", 512), ("vr", 1024), ("gr", 1024),
               ("ga", 1024), ("gb", 1024)):
    OFF[_n] = _o
    _o += _w
CHUNKS = [(0, 384), (384, 384), (768, 320)]
DOWN_BANKS = [5, 6, 7, 3, 4]
LOG_G = np.log(1.0 - 2.0 ** (-5.0 - np.arange(HR)))
CD_PROMPT = [float(np.exp(P * g)) for g in LOG_G]
CD_SAMPLE = [float(np.exp(DT * g)) for g in LOG_G]


def rows_of(t):
    return P if t < NT - 1 else SR


def parts_of(G):
    return [(0, 3, P)] if G < NG - 1 else [(0, 2, P), (2, 1, SR)]


def tokens_of(G):
    return TG if G < NG - 1 else 2 * P + SR


def units_of(G):
    return [(t, n) for t in range(3 if G < NG - 1 else 2) for n in range(HKV)]


def build_timeline(G):
    last = G == NG - 1

    def su(h, half):
        return [("SU" + "ab"[half], h)] if last else []

    s = [("P", 0), ("G", 0)]
    if G:
        s += [("LNH-", t) for t in range(3)]
    s += [("TR", 0), ("SKV", 0)]
    for h in range(1, HR):
        s += [("P", h), ("PVQ", h - 1), ("G", h)] + su(h - 1, 0) + [("TR", h)]
        if h >= 2:
            s.append(("B", h - 2))
        s += su(h - 1, 1) + [("T", h - 1), ("SKV", h)]
    s += [("GB", 0), ("GB", 1), ("PVQ", 3), ("GB", 2)] + su(3, 0) + [("B", 2)] + su(3, 1)
    s += [("GB", 3), ("T", 3), ("GB", 4), ("B", 3), ("GB", 5), ("GB", 6), ("GB", 7),
          ("MB", 0), ("KVA", 0), ("QA", 0), ("TRK", 0)]
    if last:
        s.append(("KC", 0))
    ga = [("GA", f) for f in range(KT)]

    def gate():
        return [ga.pop(0)] if ga else []

    s += gate() + gate() + [("TRQ", 0), ("TRQ", 1), ("TRQ", 2)]
    nu = len(units_of(G))
    s += [("AS", 0)] + gate() + [("AS", 1)] + gate()
    for u in range(nu):
        s.append(("AP", u))
        if u + 2 < nu:
            s.append(("AS", u + 2))
        elif last and u + 2 == nu:
            s.append(("SS", 0))
        s.append(("AV", u))
        s += gate()
    if last:
        s += [("SP", 0), ("SV", 0)]
    s += ga
    s += [("A", 0), ("A", 1), ("WO", 0)]
    if last:
        s += [("A", 2), ("WO", 1), ("A", 3), ("WO", 2)] + [("XF", t) for t in range(3)] + [("WO", 3)]
        s += [("XF", t) for t in range(3, 6)] + [("LNS", t) for t in range(3)] + [("LNH", t) for t in range(3)]
    else:
        s += [("XT+", 0), ("A", 2), ("WO", 1), ("XT+", 1), ("A", 3), ("WO", 2), ("XT+", 2), ("WO", 3)]
        s += [("LNS", t) for t in range(3)]
    return s


STAGE_PIECES = {"P": 4, "G": 2, "B": 2, "GB": 1, "GA": 1, "QA": 4, "KVA": 2, "A": 1, "WO": 2}


def numbered_timeline():
    out, n = [], MIX0
    for G in range(NG):
        for kind, x in build_timeline(G):
            g = G + {"+": 1, "-": -1}.get(kind[-1], 0)
            out.append((kind.strip("+-"), g, x, n))
            n += STAGE_PIECES.get(kind, 0)
        assert n == MIX0 + (G + 1) * NP_PHASE
    return out


TIMELINE = numbered_timeline()


def xt_base(v):
    if v < NT:
        return 3 + 2 * (v % 2)
    if v < NT + 3:
        return 0
    if v < 2 * NT:
        return 0 if (v - NT) % 3 == 1 else 3
    if v < 2 * NT + 6:
        return 3 * (v % 2)
    return 3 + 2 * (v % 2)


def slot_of(n):
    if n < MIX0:
        return n % FSLOTS
    if n < FFN2_0:
        return (n - MIX0) % MSLOTS
    return (n - FFN2_0 + (FFN2_0 - MIX0) % MSLOTS) % FSLOTS


def last_user(n):
    if n >= FFN2_0 and slot_of(n) >= MSLOTS and n < FFN2_0 + FSLOTS:
        return FFN2_0 - 1
    m = n - 1
    while m >= 0 and slot_of(m) != slot_of(n):
        m -= 1
    return m


def piece_sources(w):
    def cols(src, off, width, k0, nk):
        return src.rearrange("(k p) n -> p k n", p=P)[:, k0:k0 + nk, off:off + width]

    out = [None] * NPIECES
    for G_, kind, x, n in [(G, k, x, n) for k, G, x, n in TIMELINE]:
        for i in range(STAGE_PIECES.get(kind, 0)):
            if kind == "P":
                out[n + i] = [(512, 0, cols(w["w_in"], OFF["qr"] + x * DK, DK, 2 * i, 2)),
                              (512, DK, cols(w["w_in"], OFF["kr"] + x * DK, DK, 2 * i, 2)),
                              (512, 2 * DK, cols(w["w_in"], OFF["vr"] + x * DV, DV, 2 * i, 2))]
            elif kind == "QA":
                out[n + i] = [(512, 0, cols(w["w_in"], OFF["qa"], 512, 2 * i, 2))]
            elif kind == "G":
                out[n + i] = [(256, 0, cols(w["w_in"], OFF["gr"] + x * DV, DV, 4 * i, 4))]
            elif kind == "KVA":
                out[n + i] = [(256, 0, cols(w["w_in"], OFF["ka"], 256, 4 * i, 4))]
            elif kind in ("GA", "GB"):
                out[n + i] = [(P, 0, cols(w["w_in"], OFF[kind.lower()] + x * P, P, 0, KT))]
            elif kind == "B":
                r = x * DV + i * P
                out[n + i] = [(D, 0, w["w_br_ret"][r:r + P, :].rearrange("p (k n) -> p k n", k=1))]
            elif kind == "A":
                out[n + i] = [(256, 0, cols(w["w_br_attn"], x * 256, 256, 0, 4))]
            elif kind == "WO":
                r = (2 * x + i) * P
                out[n + i] = [(D, 0, w["w_o"][r:r + P, :].rearrange("p (k n) -> p k n", k=1))]
    return out


def raw_counts(sources):
    total, out = [0] * RAW, []
    for n in range(NPIECES):
        total[n % RAW] += 16 * (len(sources[n]) if sources[n] else 1)
        out.append(total[n % RAW])
    return out


def hybrid_layer(nc, w, c, o):
    sources = piece_sources(w)
    RAW_AT = raw_counts(sources)

    with ExitStack() as ctx:
        def sem(name):
            return ctx.enter_context(nc.semaphore(name))

        def sb(name, cols, dt=F32, stack=ctx):
            return stack.enter_context(nc.sbuf_tensor(name, [P, cols], dt))

        y = sb("y", NT * D)
        raw = sb("raw", RAW * D)
        w_hi4, w_lo4 = sb("w_hi4", MSLOTS * D, FR), sb("w_lo4", MSLOTS * D, FR)
        ident = sb("ident", P)
        ln_g, ln_b = sb("ln_g_rows", D), sb("ln_b_rows", D)
        ret_mask = sb("ret_mask", HR * P)
        ret_mask_s = sb("ret_mask_s", HR * SR)
        kdec_t, qdec_t = sb("kdec_t", 2 * HR), sb("qdec_t", 2 * HR)
        att_mask = sb("att_mask", 2 * 2 * WIN)
        att_mask_s = sb("att_mask_s", 2 * 192)
        batch_cols = sb("batch_cols", DB * SR)
        batch_rows = sb("batch_rows", DB)
        sinks, sinks_s = sb("sinks", HQ), sb("sinks_s", HKV)
        cs_att = sb("cs_att", 3 * 2 * 32)
        cs_ret = sb("cs_ret", 3 * 2 * 64)
        neg_half = sb("neg_half", 4)
        st6, mv = sb("ln_stats", NT * 12), sb("ln_mv", NT * 2)
        ve, rs, nmr = sb("ln_ve", NT), sb("ln_rs", NT), sb("ln_nmr", NT)
        gst, gmv = sb("gn_stats", 18), sb("gn_mv", 6)
        gve, grs = sb("gn_ve", 3), sb("gn_rs", 3)
        mx, nmx, esd, es, rsum, den, rden = [sb(n, 8) for n in ("mx", "nmx", "esd", "es", "rsum", "den", "rden")]
        ps = ctx.enter_context(nc.psum_tensor("ps", [P, 8 * BANK], F32))

        with ExitStack() as f:
            xT_hi, xT_lo = sb("xT_hi", KT * T, FR, f), sb("xT_lo", KT * T, FR, f)
            h_hi, h_lo = sb("h_hi", 2 * T, FR, f), sb("h_lo", 2 * T, FR, f)
            hs = sb("hs", T, F32, f)
            w_hi2, w_lo2 = sb("w_hi2", 2 * D, FR, f), sb("w_lo2", 2 * D, FR, f)
        m = ctx.enter_context(ExitStack())
        xg_hi, xg_lo = sb("xg_hi", KT * TG, FR, m), sb("xg_lo", KT * TG, FR, m)
        racc = sb("racc", KT * TG, F32, m)
        sig = sb("sig", KT * TG, F32, m)
        rst = sb("rst", 5 * DV, F32, m)
        ka_prev, va_prev = sb("ka_prev", P, F32, m), sb("va_prev", P, F32, m)
        tA, tB = sb("tA", 512, F32, m), sb("tB", 512, F32, m)
        with ExitStack() as r:
            qk = sb("qk", 3 * 2 * DK, F32, r)
            kdec = sb("kdec", 2 * 3 * DK, F32, r)
            v_r = sb("v_r", 2 * 3 * DV, F32, r)
            gs = sb("gs", 2 * 3 * DV, F32, r)
            qT, kT = sb("qT", TG, F32, r), sb("kT", TG, F32, r)
            pt_r = sb("pt_r", TG, F32, r)
            r12 = sb("r12", 2 * DV, F32, r)
            orow = sb("orow", 3 * DV, F32, r)
            orT_hi, orT_lo = sb("orT_hi", 2 * TG, FR, r), sb("orT_lo", 2 * TG, FR, r)
            st = sb("st", DB * DV, F32, r)
            kdec_m = sb("kdec_m", 4 * DK, F32, r)
            qT_m = sb("qT_m", DB * SR, F32, r)
        with ExitStack() as a:
            qa = sb("qa", 2 * 512, F32, a)
            ka = sb("ka", 3 * P, F32, a)
            qaT = sb("qaT", 3 * 512, F32, a)
            kaT, va = sb("kaT", 4 * P, F32, a), sb("va", 4 * P, F32, a)
            oaT_hi, oaT_lo = sb("oaT_hi", 4 * TG, FR, a), sb("oaT_lo", 4 * TG, FR, a)
            kcT, vc = sb("kcT", DB * P, F32, a), sb("vc", DB * P, F32, a)
            with ExitStack() as a1:
                prob = sb("prob", 2 * 1024, F32, a1)
                probT = sb("probT", 1024, F32, a1)
            mT_hi, mT_lo = sb("mT_hi", 4 * TG, FR, a), sb("mT_lo", 4 * TG, FR, a)

        raw_loaded = [sem(f"raw_loaded{i}") for i in range(RAW)]
        hi_ready, lo_ready = sem("hi_ready"), sem("lo_ready")
        piece_used = sem("piece_used")
        x_loaded = [sem(f"x_loaded{t}") for t in range(NT)]
        const_loaded, ident_loaded = sem("const_loaded"), sem("ident_loaded")
        ln_affine_v = sem("ln_affine_v")
        ln_rows_loaded = sem("ln_rows_loaded")
        cs_loaded = sem("cs_loaded")
        xt_done, xT_hi_ready, xT_lo_ready = sem("xt_done"), sem("xT_hi_ready"), sem("xT_lo_ready")
        y_scaled = sem("y_scaled")
        silu_done, h_mul, h_hi_ready, h_lo_ready = [sem(n) for n in ("silu_done", "h_mul", "h_hi_ready", "h_lo_ready")]
        down_done, acc_done = sem("down_done"), sem("acc_done")
        ln_aggr, ln_rstd, ln_hat, ln_affine = [sem(n) for n in ("ln_aggr", "ln_rstd", "ln_hat", "ln_affine")]
        dve_step, pool_step, act_step = sem("dve_step"), sem("pool_step"), sem("act_step")
        rope_read, v_ready, qk_ready, kdec_ready = [sem(n) for n in ("rope_read", "v_ready", "qk_ready", "kdec_ready")]
        gs_ready, tr_done, qkT_ready = sem("gs_ready"), sem("tr_done"), sem("qkT_ready")
        s_done, pt_ready, kv_done, r_ready = sem("s_done"), sem("pt_ready"), sem("kv_done"), sem("r_ready")
        pvq_done, o_ready, gn_aggr, gn_rstd, gn_done = [sem(n) for n in ("pvq_done", "o_ready", "gn_aggr", "gn_rstd", "gn_done")]
        t_done, or_hi_ready, or_lo_ready = sem("t_done"), sem("or_hi_ready"), sem("or_lo_ready")
        b_done, racc_done, sig_done, mb_done = sem("b_done"), sem("racc_done"), sem("sig_done"), sem("mb_done")
        st_loaded, qTm_ready, kdm_ready, su_done, st_ready, st_stored = [
            sem(n) for n in ("st_loaded", "qTm_ready", "kdm_ready", "su_done", "st_ready", "st_stored")]
        va_ready, ka_ready, trk_done, kaT_ready = [sem(n) for n in ("va_ready", "ka_ready", "trk_done", "kaT_ready")]
        qa_ready, trq_done, qaT_ready = sem("qa_ready"), sem("trq_done"), sem("qaT_ready")
        as_done, sm_read, nmx_ready, exp_done, p_ready = [sem(n) for n in ("as_done", "sm_read", "nmx_ready", "exp_done", "p_ready")]
        ap_done, pT_ready, av_done, oa_hi_ready, oa_lo_ready = [
            sem(n) for n in ("ap_done", "pT_ready", "av_done", "oa_hi_ready", "oa_lo_ready")]
        kc_loaded, vc_loaded, kc_tr, kcT_ready = sem("kc_loaded"), sem("vc_loaded"), sem("kc_tr"), sem("kcT_ready")
        m_ready, m_hi_ready, m_lo_ready = sem("m_ready"), sem("m_hi_ready"), sem("m_lo_ready")
        wo_done, wacc_done = sem("wo_done"), sem("wacc_done")
        prev_zeroed = sem("prev_zeroed")
        out_stored = sem("out_stored")
        y_stored = sem("y_stored")

        def wslot(n, lo):
            s = slot_of(n)
            if s < MSLOTS:
                return (w_lo4 if lo else w_hi4)[:, s * D:(s + 1) * D]
            return (w_lo2 if lo else w_hi2)[:, (s - MSLOTS) * D:(s - MSLOTS + 1) * D]

        def wait_affine(eng, k, t):
            mine, n = affine_count(k, t)
            eng.wait_ge(ln_affine_v if mine else ln_affine, n)

        def fr(ap):
            return ap.bitcast(F32)

        def y_tile(t):
            return y[0:rows_of(t), t * D:(t + 1) * D]

        def bank(b, rows=P, off=0, n=BANK):
            return ps[0:rows, b * BANK + off:b * BANK + off + n]

        def split_hi(eng, n, i=0, step=0):
            eng.wait_ge(raw_loaded[n % RAW], RAW_AT[n] + 16 * (step // RAW) * i)
            before = n - FSLOTS if step else last_user(n)
            if step or before >= 0:
                eng.wait_ge(piece_used, before + 1 + step * i)
            s = n % RAW
            nc.scalar.activation(wslot(n, False), raw[:, s * D:(s + 1) * D], ACT.Copy).then_inc(hi_ready, 1)

        def split_lo(eng, n, i=0, step=0):
            eng.wait_ge(hi_ready, n + 1 + step * i)
            s = n % RAW
            nc.vector.tensor_tensor(wslot(n, True), raw[:, s * D:(s + 1) * D], fr(wslot(n, False)),
                                    ALU.subtract).then_inc(lo_ready, 1)

        def sample_heads(dst):
            for par in range(2):
                pr = slice(par * HD, (par + 1) * HD)
                for nkv in range(HKV):
                    src = ps[pr, 2 * BANK + nkv * 256:2 * BANK + (nkv + 1) * 256]\
                        .rearrange("p (b h s t) -> p h s b t", b=DB, h=2, s=2)[:, :, par]
                    out = dst[pr, 2 * nkv * TG:(2 * nkv + 2) * TG].rearrange("p (h c) -> p h c", h=2)[:, :, 2 * P:2 * P + SR]
                    yield par, nkv, src, out.rearrange("p h (b t) -> p h b t", b=DB)

        class Pace:
            def __init__(self, eng, split, start):
                self.eng, self.split, self.n = eng, split, start

            def upto(self, n):
                while self.n < min(n, NPIECES):
                    self.split(self.eng, self.n)
                    self.n += 1

            def stage(self, first, count):
                ahead = AHEAD_M if first + count < FFN2_0 - 3 else 2
                held = count if count == 2 else 1
                self.upto(first + count + ahead - held + 1 if count != 2 else first + 2 + MSLOTS - 2)

        block = ctx.enter_context(nc.Block())

        @block.sync
        def _(sp):
            def load_x(t):
                src = w["x_prompt"][0, t * P:(t + 1) * P, :] if t < NT - 1 else w["x_sample"].rearrange("b t d -> (b t) d")
                sp.dma_start(y_tile(t), src).then_inc(x_loaded[t], 16)

            def raw_free(n, i=0, step=0):
                if step or n >= RAW:
                    sp.wait_ge(lo_ready, n - RAW + 1 + step * i)

            def load_ffn(f, base, i, peeled):
                wi = w["ffn_wi"][0, f].rearrange("(k p) n -> p k n", p=P)
                wo = w["ffn_wo"][0, f]
                step = 0 if peeled else 6
                todo = [(0, DFF), (1, 0), (1, DFF), (2, 0)] + [(0, None), (1, None)]
                n = base + 1 + (6 * i if peeled else 0)
                for dj, off in todo:
                    if off == 0 and dj == 2 and peeled and i == NI - 1:
                        continue
                    raw_free(n, i, step)
                    s = n % RAW
                    dst = raw[:, s * D:(s + 1) * D]
                    j = i * 2 + dj
                    if off is None:
                        sp.dma_start(dst, wo[j * P:(j + 1) * P, :] if peeled else wo[bass.ds(j * P, P), :])\
                          .then_inc(raw_loaded[s], 16)
                    else:
                        src = wi[:, :, off + j * P:off + (j + 1) * P] if peeled else wi[:, :, bass.ds(j * P + off, P)]
                        sp.dma_start(dst.rearrange("p (k n) -> p k n", k=KT), src).then_inc(raw_loaded[s], 16)
                    n += 1

            def load_ffn_phase(f, base):
                wi = w["ffn_wi"][0, f].rearrange("(k p) n -> p k n", p=P)
                raw_free(base)
                if f == 0:
                    for t in range(3):
                        load_x(t)
                sp.dma_start(raw[:, 0:D].rearrange("p (k n) -> p k n", k=KT), wi[:, :, 0:P]).then_inc(raw_loaded[0], 16)
                if f == 0:
                    for t in range(3, NT):
                        load_x(t)
                load_ffn(f, base, 0, True)
                with sp.Fori(1, NI - 1) as i:
                    load_ffn(f, base, i, False)
                load_ffn(f, base, NI - 1, True)

            load_ffn_phase(0, 0)
            for n in range(MIX0, FFN2_0):
                raw_free(n)
                s = n % RAW
                for width, off, src in sources[n]:
                    k, cols = src.shape[1], src.shape[2]
                    dst = raw[:, s * D:(s + 1) * D].rearrange("p (k n) -> p k n", n=width)[:, 0:k, off:off + cols]
                    sp.dma_start(dst, src).then_inc(raw_loaded[s], 16)
            load_ffn_phase(1, FFN2_0)
            for t in range(NT):
                wait_affine(sp, 2, t)
                dst = o["y_prompt"][0, t * P:(t + 1) * P, :] if t < NT - 1 else o["y_sample"].rearrange("b t d -> (b t) d")
                sp.dma_start(dst, y_tile(t)).then_inc(y_stored, 16)
            sp.wait_ge(y_stored, 16 * NT)

        @block.gpsimd
        def _(pool):
            step = [0]

            def link(ins):
                step[0] += 1
                ins.then_inc(pool_step, 1)
                pool.wait_ge(pool_step, step[0])

            link(nc.gpsimd.memset(neg_half[:], -0.5))
            n_out = [0]

            def store(dst, src):
                pool.dma_start(dst, src).then_inc(out_stored, 16)
                n_out[0] += 1

            keep = WIN - DT
            for name, cache in (("kcs", "cache_k"), ("vcs", "cache_v")):
                store(o[name][0, :, 0:keep].rearrange("b w n d -> b (w n d)"),
                      w[cache][0, :, DT:WIN].rearrange("b w n d -> b (w n d)"))

            def load_ln_rows(k):
                if k:
                    pool.wait_ge(pool_step, step[0])
                pool.dma_start(ln_g[:], w["ln_g"][0, k:k + 1, :].to_broadcast([P, D])).then_inc(ln_rows_loaded, 16)
                pool.dma_start(ln_b[:], w["ln_b"][0, k:k + 1, :].to_broadcast([P, D])).then_inc(ln_rows_loaded, 16)

            load_ln_rows(0)

            def rstd(idx, t):
                R = rows_of(t)
                pool.wait_ge(ln_aggr, idx + 1)
                link(nc.gpsimd.tensor_scalar(ve[0:R, t:t + 1], mv[0:R, 2 * t + 1:2 * t + 2], LN_EPS, None, ALU.add))
                link(nc.gpsimd.tensor_tensor(rs[0:R, t:t + 1], ve[0:R, t:t + 1], neg_half[0:R, 0:1], ALU.pow))
                nc.gpsimd.tensor_scalar(nmr[0:R, t:t + 1], mv[0:R, 2 * t:2 * t + 1], rs[0:R, t:t + 1], -1.0,
                                        ALU.mult, ALU.mult).then_inc(ln_rstd, 1)

            def affine(idx, t, k):
                R = rows_of(t)
                pool.wait_ge(ln_rows_loaded, 32 * (k + 1))
                pool.wait_ge(ln_hat, idx + 1)
                link(nc.gpsimd.tensor_tensor(y_tile(t), y_tile(t), ln_g[0:R, :], ALU.mult))
                nc.gpsimd.tensor_tensor(y_tile(t), y_tile(t), ln_b[0:R, :], ALU.add).then_inc(ln_affine, 1)

            def scale_y(v, t):
                pool.wait_ge(xt_done, v + 1)
                nc.gpsimd.tensor_scalar(y_tile(t), y_tile(t), ALPHA, None, ALU.mult).then_inc(y_scaled, 1)

            def ln_all(k):
                todo = list(range(NT))
                for t in range(NT):
                    while todo and todo[0] <= 2 * t:
                        rstd(k * NT + todo[0], todo.pop(0))
                    if t not in DVE_AFFINE[k]:
                        affine(k * NT + t, t, k)

            def load_cs(G):
                pool.dma_start(cs_att[:], c["cs_att"][:, G]).then_inc(cs_loaded, 16)
                pool.dma_start(cs_ret[:], c["cs_ret"][:, G]).then_inc(cs_loaded, 16)

            load_cs(0)
            for t in range(NT):
                scale_y(t, t)
            ln_all(0)
            for t in range(3):
                scale_y(NT + t, t)
            pool.wait_ge(ln_affine, NT)
            load_ln_rows(1)
            for kind, G, x, n in TIMELINE:
                g = HR * G + x
                if kind == "XT":
                    if x == 0:
                        pool.wait_ge(qa_ready, 3 * G)
                        load_cs(G)
                    scale_y(NT + 3 * G + x, 3 * G + x)
                elif kind == "XF":
                    scale_y(2 * NT + x, x)
                elif kind == "P" and G == NG - 1 and x == 0:
                    pool.wait_ge(piece_used, n)
                    pool.dma_start(st[:].rearrange("p (b e) -> p b e", b=DB),
                                   w["state_ret"][0, :, 0].rearrange("b p e -> p b e")).then_inc(st_loaded, 16)
                elif kind == "PVQ":
                    pool.wait_ge(gn_aggr, g + 1)
                    for i, (t0, nt, R) in enumerate(parts_of(G)):
                        link(nc.gpsimd.tensor_scalar(gve[0:R, t0:t0 + nt],
                                                     gmv[0:R, :].rearrange("p (t s) -> p t s", s=2)[:, t0:t0 + nt, 1],
                                                     GN_EPS, None, ALU.add))
                        for t in range(t0, t0 + nt):
                            ins = nc.gpsimd.tensor_tensor(grs[0:R, t:t + 1], gve[0:R, t:t + 1], neg_half[0:R, 0:1], ALU.pow)
                    ins.then_inc(gn_rstd, 1)
                elif kind == "SUb":
                    pool.wait_ge(st_ready, 2 * (x + 1))
                    pool.dma_start(o["rs"][0, :, x].rearrange("b p e -> p b e"),
                                   st[:].rearrange("p (b e) -> p b e", b=DB)).then_inc(st_stored, 16)
                    if x < HR - 1:
                        pool.wait_ge(st_stored, 16 * (x + 1))
                        pool.dma_start(st[:].rearrange("p (b e) -> p b e", b=DB),
                                       w["state_ret"][0, :, x + 1].rearrange("b p e -> p b e")).then_inc(st_loaded, 16)
                    slot = (x - NG) % 5
                    store(o["rp"][0, 0, x], rst[:, slot * DV:(slot + 1) * DV])
                elif kind == "KVA" and G == NG - 1:
                    pool.wait_ge(piece_used, n)
                    pool.wait_ge(st_stored, 16 * HR)
                    pool.dma_start(prob[:, 0:1024].rearrange("p (b e) -> p b e", b=DB),
                                   w["cache_k"][0].rearrange("b w n d -> w b (n d)")).then_inc(kc_loaded, 16)
                    pool.dma_start(vc[:].rearrange("p (b e) -> p b e", b=DB),
                                   w["cache_v"][0].rearrange("b w n d -> w b (n d)")).then_inc(vc_loaded, 16)
                elif kind == "TRK" and G == NG - 1:
                    pool.wait_ge(ka_ready, NG)
                    pool.wait_ge(va_ready, NG)
                    store(o["kcp"][0, 0].rearrange("w n d -> w (n d)"), ka[:, P:2 * P])
                    store(o["vcp"][0, 0].rearrange("w n d -> w (n d)"), va[:, 2 * P:3 * P])
                    for b in range(DB):
                        store(o["kcs"][0, b, keep:WIN].rearrange("w n d -> w (n d)"), ka[b * DT:(b + 1) * DT, 2 * P:3 * P])
                        store(o["vcs"][0, b, keep:WIN].rearrange("w n d -> w (n d)"), va[b * DT:(b + 1) * DT, 3 * P:4 * P])
                elif kind == "LNS":
                    rstd(NT + 3 * G + x, 3 * G + x)
                elif kind == "LNH":
                    if 3 * G + x not in DVE_AFFINE[1]:
                        affine(NT + 3 * G + x, 3 * G + x, 1)
            for t in range(6, NT):
                scale_y(2 * NT + t, t)
            for t in (5, NT - 1):
                wait_affine(pool, 1, t)
            load_ln_rows(2)
            ln_all(2)
            pool.wait_ge(out_stored, 16 * n_out[0])
            pool.wait_ge(st_stored, 16 * HR)

        @block.scalar
        def _(act):
            consts = [(ret_mask, c["ret_mask"]), (kdec_t, c["kdec_t"]), (qdec_t, c["qdec_t"]),
                      (att_mask, c["att_mask"]), (att_mask_s, c["att_mask_s"]), (batch_cols, c["batch_cols"]),
                      (sinks, c["sinks"]), (sinks_s, c["sinks_s"])]
            act.dma_start(ident[:], c["ident"]).then_inc(ident_loaded, 16)
            for dst, src in consts:
                act.dma_start(dst[:], src).then_inc(const_loaded, 16)
            for dst, src in ((ret_mask_s, c["ret_mask_s"]), (batch_rows, c["batch_rows"])):
                act.dma_start(dst[0:SR, :], src).then_inc(const_loaded, 16)

            def xT_evac(v, t, dst, width, col):
                R = rows_of(t)
                act.wait_ge(xt_done, v + 1)
                pair = ps[:, xt_base(v) * BANK:][:, 0:KT * P].rearrange("p (k c) -> p k c", k=KT)[:, :, 0:R]
                out = dst[:].rearrange("p (k c) -> p k c", c=width)[:, :, col:col + R]
                nc.scalar.activation(out, pair, ACT.Copy).then_inc(xT_hi_ready, 1)

            def hat(idx, t):
                R = rows_of(t)
                act.wait_ge(ln_rstd, idx + 1)
                nc.scalar.activation(y_tile(t), y_tile(t), ACT.Identity, bias=nmr[0:R, t:t + 1],
                                     scale=rs[0:R, t:t + 1]).then_inc(ln_hat, 1)

            def ffn(f, base):
                J0, I0 = NJ * f, NI * f

                def silu(jexpr, n, i, st):
                    act.wait_ge(piece_used, n + 1 + st * i)
                    if not (isinstance(jexpr, int) and jexpr == 0):
                        act.wait_ge(h_lo_ready, jexpr * 3)
                    for ci, (c0, cw) in enumerate(CHUNKS):
                        nc.scalar.activation(hs[:, c0:c0 + cw], bank(ci, n=cw), ACT.Silu).then_inc(silu_done, 1)

                def h_round(jexpr, slot, prior):
                    if prior is not None:
                        act.wait_ge(piece_used, prior)
                    for ci, (c0, cw) in enumerate(CHUNKS):
                        act.wait_ge(h_mul, jexpr * 3 + ci + 1)
                        nc.scalar.activation(h_hi[:, slot * T + c0:slot * T + c0 + cw], hs[:, c0:c0 + cw],
                                             ACT.Copy).then_inc(h_hi_ready, 1)

                def turn(i, peeled):
                    st = 0 if peeled else 6
                    n = base + 1 + (6 * i if peeled else 0)
                    J = i * 2 + J0
                    lastt = peeled and i == NI - 1

                    def split(k):
                        if not peeled:
                            split_hi(act, n + k + AHEAD_F, i, 6)
                        else:
                            pace.upto(n + k + AHEAD_F + 1)
                    prior = None if (peeled and i == 0) else (base + 1 + 6 * i)
                    split(0)
                    h_round(J, 0, prior)
                    split(1)
                    silu(J + 1, n + 1, i, st)
                    split(2)
                    h_round(J + 1, 1, prior)
                    split(3)
                    if not lastt:
                        silu(J + 2, n + 3, i, st)
                        split(4)
                        split(5)

                pace.upto(base + AHEAD_F + 1)
                silu(J0, base, 0, 0)
                turn(0, True)
                with act.Fori(1, NI - 1) as i:
                    turn(i, False)
                pace.n = base + 1 + 6 * (NI - 1) + AHEAD_F
                turn(NI - 1, True)

            pace = Pace(act, split_hi, 0)
            pace.upto(1)
            for t in range(3):
                xT_evac(t, t, xT_hi, T, t * P)
            pace.upto(AHEAD_F)
            for t in range(3, NT):
                xT_evac(t, t, xT_hi, T, t * P)
            ffn(0, 0)
            pace.upto(MIX0 + MSLOTS)
            for t in range(NT):
                hat(t, t)
                if t >= 6:
                    xT_evac(NT + t - 6, t - 6, xg_hi, TG, (t - 6) * P)
            act.wait_ge(const_loaded, 16 * (len(consts) + 2))

            chain = [0]

            def link(ins):
                chain[0] += 1
                ins.then_inc(act_step, 1)
                act.wait_ge(act_step, chain[0])

            n_unit = [0]
            n_tile = [0]
            for kind, G, x, n in TIMELINE:
                g = HR * G + x
                TGn = tokens_of(G)
                k = STAGE_PIECES.get(kind, 0)
                if k:
                    pace.stage(n, k)
                if kind == "XT":
                    xT_evac(NT + 3 * G + x, 3 * G + x, xg_hi, TG, x * P)
                elif kind == "XF":
                    if x == 0:
                        act.wait_ge(st_stored, 16 * HR)
                        act.wait_ge(out_stored, 16 * (2 + HR + 2 + 2 * DB))
                    xT_evac(2 * NT + x, x, xT_hi, T, x * P)
                elif kind == "P":
                    act.wait_ge(rope_read, g + 1)
                    if g >= 2:
                        act.wait_ge(pvq_done, g - 1)
                        if G == NG - 1 and x >= 2:
                            act.wait_ge(su_done, 2 * (x - 1))
                    for t0, nt, R in parts_of(G):
                        src = ps[0:R, 0:3 * BANK].rearrange("p (t c) -> p t c", t=3)[:, t0:t0 + nt, 2 * DK:]
                        dst = v_r[0:R, (g % 2) * 3 * DV:(g % 2 + 1) * 3 * DV].rearrange("p (t c) -> p t c", t=3)[:, t0:t0 + nt, :]
                        ins = nc.scalar.activation(dst, src, ACT.Copy)
                    ins.then_inc(v_ready, 1)
                elif kind == "G":
                    act.wait_ge(piece_used, n + 2)
                    if g >= 2:
                        act.wait_ge(gn_done, g - 1)
                    for t0, nt, R in parts_of(G):
                        src = ps[0:R, 3 * BANK:6 * BANK].rearrange("p (t c) -> p t c", t=3)[:, t0:t0 + nt, 0:DV]
                        dst = gs[0:R, (g % 2) * 3 * DV:(g % 2 + 1) * 3 * DV].rearrange("p (t c) -> p t c", t=3)[:, t0:t0 + nt, :]
                        ins = nc.scalar.activation(dst, src, ACT.Silu)
                    ins.then_inc(gs_ready, 1)
                elif kind == "TR":
                    act.wait_ge(tr_done, g + 1)
                    if g:
                        act.wait_ge(pvq_done, g)
                    nc.scalar.activation(qT[:, 0:TGn], bank(0, n=TGn), ACT.Copy).then_inc(qkT_ready, 1)
                    nc.scalar.activation(kT[:, 0:TGn], bank(1, n=TGn), ACT.Copy).then_inc(qkT_ready, 1)
                elif kind == "PVQ":
                    act.wait_ge(pvq_done, g + 1)
                    if g:
                        act.wait_ge(t_done, g)
                    for i, (t0, nt, R) in enumerate(parts_of(G)):
                        ins = nc.scalar.activation(orow[0:R, t0 * DV:(t0 + nt) * DV],
                                                   ps[0:R, 6 * BANK + t0 * DV:6 * BANK + (t0 + nt) * DV], ACT.Copy,
                                                   scale=qdec_t[0:R, HR * i + x:HR * i + x + 1])
                    ins.then_inc(o_ready, 1)
                elif kind == "T":
                    act.wait_ge(t_done, g + 1)
                    b = 4 if x < HR - 1 else 6
                    src = ps[:, b * BANK:(b + 2) * BANK].rearrange("p (e c) -> p e c", e=2)[:, :, 0:TGn]
                    dst = orT_hi[:].rearrange("p (e c) -> p e c", e=2)[:, :, 0:TGn]
                    nc.scalar.activation(dst, src, ACT.Copy).then_inc(or_hi_ready, 1)
                elif kind in ("GB", "GA"):
                    act.wait_ge(piece_used, n + 1)
                    b = 3 + (x + 1) % 3 if kind == "GB" else 6 + x % 2
                    if kind == "GA":
                        act.wait_ge(mb_done, KT * G + x + 1)
                    elif G:
                        act.wait_ge(m_lo_ready, 4 * G)
                    nc.scalar.activation(sig[:, x * TG:x * TG + TGn], bank(b, n=TGn), ACT.Sigmoid).then_inc(sig_done, 1)
                elif kind == "KVA":
                    act.wait_ge(ka_ready, G + 1)
                    if G == 0:
                        act.wait_ge(prev_zeroed, 2)
                    link(nc.scalar.activation(va[:, 0:P], va_prev[:], ACT.Copy))
                    for t0, nt, R in parts_of(G):
                        src = ps[0:R, 3 * BANK:6 * BANK].rearrange("p (t c) -> p t c", t=3)[:, t0:t0 + nt, P:2 * P]
                        dst = va[0:R, P:].rearrange("p (t c) -> p t c", t=3)[:, t0:t0 + nt, :]
                        ins = nc.scalar.activation(dst, src, ACT.Copy)
                    ins.then_inc(va_ready, 1)
                    if G < NG - 1:
                        act.wait_ge(va_ready, G + 1)
                        link(nc.scalar.activation(va_prev[:], va[:, 3 * P:4 * P], ACT.Copy))
                elif kind == "TRK":
                    act.wait_ge(trk_done, G + 1)
                    link(nc.scalar.activation(kaT[:, 0:P], ka_prev[:], ACT.Copy))
                    nc.scalar.activation(kaT[:, P:P + TGn], bank(5, n=TGn), ACT.Copy).then_inc(kaT_ready, 1)
                    if G < NG - 1:
                        act.wait_ge(kaT_ready, G + 1)
                        link(nc.scalar.activation(ka_prev[:], kaT[:, 3 * P:4 * P], ACT.Copy))
                elif kind == "TRQ":
                    R = rows_of(3 * G + x)
                    act.wait_ge(trq_done, 3 * G + x + 1)
                    src = bank(3 + x).rearrange("p (g c) -> p g c", g=GQ)[:, :, 0:R]
                    if R == P:
                        dst = qaT[:, x * 512:(x + 1) * 512].rearrange("p (g c) -> p g c", g=GQ)
                    else:
                        src = src.rearrange("p g (b t) -> p g b t", b=DB)
                        dst = qaT[:, x * 512:x * 512 + GQ * SR].rearrange("p (b g t) -> p g b t", b=DB, g=GQ)
                    nc.scalar.activation(dst, src, ACT.Copy).then_inc(qaT_ready, 1)
                elif kind == "KC":
                    act.wait_ge(kc_tr, 1)
                    nc.scalar.activation(kcT[:], ps[:, 6 * BANK:8 * BANK], ACT.Copy).then_inc(kcT_ready, 1)
                elif kind in ("AS", "SS"):
                    u = n_unit[0]
                    act.wait_ge(nmx_ready, u + 1)
                    nc.scalar.activation(es[:, 0:4], esd[:, 0:4], ACT.Exp)
                    wd = 2 * WIN if kind == "AS" else 192
                    pb = prob[:, (u % 2) * 1024:(u % 2) * 1024 + 4 * wd]
                    for q in range(4):
                        ins = nc.scalar.activation(pb[:, q * wd:(q + 1) * wd], pb[:, q * wd:(q + 1) * wd], ACT.Exp,
                                                   bias=nmx[:, q:q + 1], accum_out=rsum[:, q:q + 1])
                    ins.then_inc(exp_done, 1)
                    n_unit[0] += 1
                elif kind in ("AP", "SP"):
                    u = n_unit[0] if kind == "SP" else (len(units_of(0)) * G + x + 1)
                    act.wait_ge(ap_done, u)
                    if u >= 2:
                        act.wait_ge(av_done, u - 1)
                    if kind == "AP":
                        nc.scalar.activation(probT[:], ps[:, 0:2 * BANK], ACT.Copy).then_inc(pT_ready, 1)
                    else:
                        nc.scalar.activation(probT[:, 0:512], bank(0), ACT.Copy)
                        nc.scalar.activation(probT[0:SR, 512:1024], bank(1, SR), ACT.Copy).then_inc(pT_ready, 1)
                elif (kind == "AV" and x % 2 == 1) or kind == "SV":
                    u = len(units_of(0)) * G + x + 1 if kind == "AV" else len(units_of(0)) * G + 5
                    t = x // 2 if kind == "AV" else 2
                    R = rows_of(3 * G + t)
                    act.wait_ge(av_done, u)
                    if kind == "SV":
                        for par, nkv, src, dst in sample_heads(oaT_hi):
                            ins = nc.scalar.activation(dst, src, ACT.Copy)
                        ins.then_inc(oa_hi_ready, 1)
                        continue
                    nc.scalar.activation(oaT_hi[:].rearrange("p (k c) -> p k c", k=4)[:, :, t * P:t * P + R],
                                         bank(2).rearrange("p (k c) -> p k c", k=4)[:, :, 0:R], ACT.Copy).then_inc(oa_hi_ready, 1)
                elif kind == "A":
                    act.wait_ge(m_ready, KT * G + 2 * x + 2)
                    if x >= 2:
                        wo_n = [nn for kk, gg, xx, nn in TIMELINE if (kk, gg, xx) == ("WO", G, x - 2)][0]
                        act.wait_ge(piece_used, wo_n + 2)
                    src = sig[:, 2 * x * TG:(2 * x + 2) * TG].rearrange("p (f c) -> p f c", f=2)[:, :, 0:TGn]
                    dst = mT_hi[:, (x % 2) * 2 * TG:(x % 2 + 1) * 2 * TG].rearrange("p (f c) -> p f c", f=2)[:, :, 0:TGn]
                    nc.scalar.activation(dst, src, ACT.Copy).then_inc(m_hi_ready, 1)
                elif kind == "LNH":
                    hat(NT + 3 * G + x, 3 * G + x)

            for t in range(6, NT):
                xT_evac(2 * NT + t, t, xT_hi, T, t * P)
            ffn(1, FFN2_0)
            for t in range(NT):
                hat(2 * NT + t, t)

        @block.vector
        def _(dve):
            step = [0]

            def link(ins):
                step[0] += 1
                ins.then_inc(dve_step, 1)
                dve.wait_ge(dve_step, step[0])

            tt = nc.vector.tensor_tensor

            def xT_evac(v, t, dst_hi, dst_lo, width, col):
                R = rows_of(t)
                dve.wait_ge(xT_hi_ready, v + 1)
                pair = ps[:, xt_base(v) * BANK:][:, 0:KT * P].rearrange("p (k c) -> p k c", k=KT)[:, :, 0:R]
                hi = fr(dst_hi[:].rearrange("p (k c) -> p k c", c=width)[:, :, col:col + R])
                lo = dst_lo[:].rearrange("p (k c) -> p k c", c=width)[:, :, col:col + R]
                tt(lo, pair, hi, ALU.subtract).then_inc(xT_lo_ready, 1)

            def ln_stats(t):
                R = rows_of(t)
                for q in range(2):
                    ins = nc.vector.bn_stats(st6[0:R, 12 * t + 6 * q:12 * t + 6 * q + 6],
                                             y[0:R, t * D + 512 * q:t * D + 512 * q + 512])
                link(ins)
                nc.vector.bn_aggr(mv[0:R, 2 * t:2 * t + 2], st6[0:R, 12 * t:12 * t + 12]).then_inc(ln_aggr, 1)

            def ffn(f, base):
                J0, I0 = NJ * f, NI * f

                def mul(jexpr, n, i, st_):
                    dve.wait_ge(piece_used, n + 1 + st_ * i)
                    for ci, (c0, cw) in enumerate(CHUNKS):
                        dve.wait_ge(silu_done, jexpr * 3 + ci + 1)
                        nc.vector.scalar_tensor_tensor(out=hs[:, c0:c0 + cw], in0=hs[:, c0:c0 + cw], scalar=0.5,
                                                       in1=bank(3 + ci, n=cw), op0=ALU.mult, op1=ALU.mult)\
                            .then_inc(h_mul, 1)

                def h_rest(jexpr, slot):
                    for ci, (c0, cw) in enumerate(CHUNKS):
                        dve.wait_ge(h_hi_ready, jexpr * 3 + ci + 1)
                        hi = h_hi[:, slot * T + c0:slot * T + c0 + cw]
                        tt(h_lo[:, slot * T + c0:slot * T + c0 + cw], hs[:, c0:c0 + cw], fr(hi), ALU.subtract)\
                            .then_inc(h_lo_ready, 1)

                def accumulate(i, n_wo, st_, first, stats):
                    for q in range(2 * NT):
                        t, half = q // 2, q % 2
                        R = rows_of(t)
                        if first and half == 0:
                            dve.wait_ge(y_scaled, 2 * NT * f + t + 1)
                        if q < 2 * NT - 1:
                            dve.wait_ge(down_done, i * 17 + I0 * 17 + q + 1)
                        else:
                            dve.wait_ge(piece_used, n_wo + 2 + st_ * i)
                        ysl = y[0:R, t * D + half * 512:t * D + half * 512 + 512]
                        tt(ysl, ysl, bank(DOWN_BANKS[q % 5], R), ALU.add).then_inc(acc_done, 1)
                        if stats and half == 1:
                            dve.wait_ge(acc_done, 18 * (I0 + i) + q + 1)
                            ln_stats(t)
                            if f == 0 and t >= 6:
                                xT_evac(NT + t - 6, t - 6, xg_hi, xg_lo, TG, (t - 6) * P)

                def turn(i, peeled):
                    st_ = 0 if peeled else 6
                    n = base + 1 + (6 * i if peeled else 0)
                    J = i * 2 + J0
                    lastt = peeled and i == NI - 1

                    def split(k):
                        if not peeled:
                            split_lo(dve, n + k + AHEAD_F, i, 6)
                        else:
                            pace.upto(n + k + AHEAD_F + 1)
                    split(0)
                    mul(J, n, i, st_)
                    h_rest(J, 0)
                    split(1)
                    split(2)
                    mul(J + 1, n + 2, i, st_)
                    h_rest(J + 1, 1)
                    split(3)
                    if not lastt:
                        split(4)
                        split(5)
                    elif f == 0:
                        pace.upto(MIX0 + MSLOTS)
                    accumulate(i, n + (3 if lastt else 4), st_, peeled and i == 0, lastt)

                pace.upto(base + AHEAD_F + 1)
                turn(0, True)
                with dve.Fori(1, NI - 1) as i:
                    turn(i, False)
                pace.n = base + 1 + 6 * (NI - 1) + AHEAD_F
                turn(NI - 1, True)

            def affine(k, t):
                R = rows_of(t)
                dve.wait_ge(ln_rows_loaded, 32 * (k + 1))
                dve.wait_ge(ln_hat, k * NT + t + 1)
                link(tt(y_tile(t), y_tile(t), ln_g[0:R, :], ALU.mult))
                tt(y_tile(t), y_tile(t), ln_b[0:R, :], ALU.add).then_inc(ln_affine_v, 1)

            pace = Pace(dve, split_lo, 0)
            pace.upto(1)
            for t in range(3):
                xT_evac(t, t, xT_hi, xT_lo, T, t * P)
            pace.upto(AHEAD_F)
            for t in range(3, NT):
                xT_evac(t, t, xT_hi, xT_lo, T, t * P)
            ffn(0, 0)
            dve.wait_ge(const_loaded, 16 * 10)
            dve.wait_ge(piece_used, MIX0)
            nc.vector.memset(ka_prev[:], 0.0).then_inc(prev_zeroed, 1)
            nc.vector.memset(va_prev[:], 0.0).then_inc(prev_zeroed, 1)

            def rope(G, R, src, t, cs, half, heads, dst1, dst2):
                cos = cs[0:R, t * 2 * half:t * 2 * half + half]
                sin = cs[0:R, t * 2 * half + half:(t + 1) * 2 * half]
                n2 = 2 * heads
                a3 = tA[0:R, 0:n2 * half].rearrange("p (h c) -> p h c", c=half)
                b3 = tB[0:R, 0:n2 * half].rearrange("p (h c) -> p h c", c=half)
                s3 = src.rearrange("p (h c) -> p h c", c=half)
                tt(a3, s3, cos.unsqueeze(1).to_broadcast([R, n2, half]), ALU.mult)
                link(tt(b3, s3, sin.unsqueeze(1).to_broadcast([R, n2, half]), ALU.mult))
                return a3, b3

            n_unit = [0]
            for kind, G, x, n in TIMELINE:
                g = HR * G + x
                TGn = tokens_of(G)
                k = STAGE_PIECES.get(kind, 0)
                if k:
                    pace.stage(n, k)
                if kind == "XT":
                    xT_evac(NT + 3 * G + x, 3 * G + x, xg_hi, xg_lo, TG, x * P)
                elif kind == "XF":
                    if x == 0:
                        dve.wait_ge(st_stored, 16 * HR)
                        dve.wait_ge(out_stored, 16 * (2 + HR + 2 + 2 * DB))
                    xT_evac(2 * NT + x, x, xT_hi, xT_lo, T, x * P)
                elif kind == "P":
                    dve.wait_ge(piece_used, n + 4)
                    if x == 0:
                        dve.wait_ge(cs_loaded, 32 * (G + 1))
                    if g:
                        dve.wait_ge(tr_done, g)
                    for t in range(3):
                        R = rows_of(3 * G + t)
                        a3, b3 = rope(G, R, bank(t, R, 0, 2 * DK), t, cs_ret, DK // 2, 2, None, None)
                        av = a3.rearrange("p (q s) c -> p q s c", s=2)
                        bv = b3.rearrange("p (q s) c -> p q s c", s=2)
                        ov = qk[0:R, t * 2 * DK:(t + 1) * 2 * DK].rearrange("p (q s c) -> p q s c", s=2, c=DK // 2)
                        tt(ov[:, :, 0, :], av[:, :, 0, :], bv[:, :, 1, :], ALU.subtract)
                        ins = tt(ov[:, :, 1, :], av[:, :, 1, :], bv[:, :, 0, :], ALU.add)
                        if t < 2:
                            link(ins)
                    ins.then_inc(rope_read, 1)
                elif kind == "G":
                    dve.wait_ge(rope_read, g + 1)
                    if g:
                        dve.wait_ge(kv_done, kv_count(G, x - 1) if x else kv_count(G - 1, HR - 1))
                    for i, (t0, nt, R) in enumerate(parts_of(G)):
                        src = qk[0:R, :].rearrange("p (t c) -> p t c", t=3)[:, t0:t0 + nt, DK:]
                        dst = kdec[0:R, (g % 2) * 3 * DK:(g % 2 + 1) * 3 * DK].rearrange("p (t c) -> p t c", t=3)[:, t0:t0 + nt, :]
                        ins = nc.vector.tensor_scalar(dst, src, kdec_t[0:R, HR * i + x:HR * i + x + 1], None, ALU.mult)
                    ins.then_inc(kdec_ready, 1)
                elif kind == "TR" and G == NG - 1:
                    dve.wait_ge(qkT_ready, 2 * g + 1)
                    tt(qT_m[:].rearrange("p (b c) -> p b c", b=DB),
                       qT[:, 2 * P:2 * P + SR].unsqueeze(1).to_broadcast([P, DB, SR]),
                       batch_cols[:].rearrange("p (b c) -> p b c", b=DB), ALU.mult).then_inc(qTm_ready, 1)
                elif kind == "SKV":
                    dve.wait_ge(s_done, g + 1)
                    for i, (t0, nt, R) in enumerate(parts_of(G)):
                        src = ps[0:R, 6 * BANK + t0 * P:6 * BANK + (t0 + nt) * P].rearrange("p (t c) -> p t c", t=nt)[:, :, 0:R]
                        dst = pt_r[0:R, t0 * P:(t0 + nt) * P].rearrange("p (t c) -> p t c", t=nt)[:, :, 0:R]
                        msk = (ret_mask[:, x * P:(x + 1) * P] if i == 0 else ret_mask_s[0:SR, x * SR:(x + 1) * SR])
                        ins = tt(dst, src, msk.unsqueeze(1).to_broadcast([R, nt, R]), ALU.mult)
                    ins.then_inc(pt_ready, 1)
                    cd = CD_PROMPT[x]
                    src_slot, dst_slot = (x - G) % 5, (x - G - 1) % 5
                    chain_in = rst[:, src_slot * DV:(src_slot + 1) * DV]
                    ntp = 3 if G < NG - 1 else 2
                    base_kv = kv_count(G, x) - (2 if G < NG - 1 else 1)
                    for t in range(ntp):
                        dve.wait_ge(kv_done, base_kv + (1 if t < 2 else 2))
                        src = bank(7, P, t * DV, DV) if t < 2 else bank(3, P, 0, DV)
                        final = t == ntp - 1
                        dst = rst[:, dst_slot * DV:(dst_slot + 1) * DV] if final else r12[:, t * DV:(t + 1) * DV]
                        if G == 0 and t == 0:
                            ins = nc.vector.tensor_copy(dst, src)
                        else:
                            ins = nc.vector.scalar_tensor_tensor(out=dst, in0=chain_in, scalar=cd, in1=src,
                                                                 op0=ALU.mult, op1=ALU.add)
                        if final:
                            ins.then_inc(r_ready, 1)
                        else:
                            link(ins)
                        chain_in = dst
                elif kind == "PVQ":
                    dve.wait_ge(o_ready, g + 1)
                    for t in range(3):
                        R = rows_of(3 * G + t)
                        ins = nc.vector.bn_stats(gst[0:R, 6 * t:6 * t + 6], orow[0:R, t * DV:(t + 1) * DV])
                    link(ins)
                    for t in range(3):
                        R = rows_of(3 * G + t)
                        ins = nc.vector.bn_aggr(gmv[0:R, 2 * t:2 * t + 2], gst[0:R, 6 * t:6 * t + 6])
                    ins.then_inc(gn_aggr, 1)
                    dve.wait_ge(gn_rstd, g + 1)
                    for t in range(3):
                        R = rows_of(3 * G + t)
                        ot = orow[0:R, t * DV:(t + 1) * DV]
                        ins = nc.vector.tensor_scalar(ot, ot, gmv[0:R, 2 * t:2 * t + 1], grs[0:R, t:t + 1],
                                                      ALU.subtract, ALU.mult)
                    link(ins)
                    dve.wait_ge(gs_ready, g + 1)
                    for t0, nt, R in parts_of(G):
                        ot = orow[0:R, t0 * DV:(t0 + nt) * DV]
                        g0 = (g % 2) * 3 * DV
                        ins = tt(ot, ot, gs[0:R, g0 + t0 * DV:g0 + (t0 + nt) * DV], ALU.mult)
                    ins.then_inc(gn_done, 1)
                elif kind in ("SUa", "SUb"):
                    for half in ([0] if kind == "SUa" else [1]):
                        if x or half:
                            dve.wait_ge(su_done, 2 * x + half)
                        tt(kdec_m[0:SR, :].rearrange("p (b c) -> p b c", b=4),
                           kdec[0:SR, (3 * (g % 2) + 2) * DK:(3 * (g % 2) + 3) * DK].unsqueeze(1).to_broadcast([SR, 4, DK]),
                           batch_rows[0:SR, 4 * half:4 * half + 4].unsqueeze(2).to_broadcast([SR, 4, DK]),
                           ALU.mult).then_inc(kdm_ready, 1)
                        dve.wait_ge(su_done, 2 * x + half + 1)
                        sl = st[:, half * 4 * DV:(half + 1) * 4 * DV]
                        nc.vector.scalar_tensor_tensor(out=sl, in0=sl, scalar=CD_SAMPLE[x], in1=ps[:, 6 * BANK:8 * BANK],
                                                       op0=ALU.mult, op1=ALU.add).then_inc(st_ready, 1)
                elif kind == "T":
                    dve.wait_ge(or_hi_ready, g + 1)
                    b = 4 if x < HR - 1 else 6
                    src = ps[:, b * BANK:(b + 2) * BANK].rearrange("p (e c) -> p e c", e=2)[:, :, 0:TGn]
                    hi = fr(orT_hi[:].rearrange("p (e c) -> p e c", e=2)[:, :, 0:TGn])
                    lo = orT_lo[:].rearrange("p (e c) -> p e c", e=2)[:, :, 0:TGn]
                    tt(lo, src, hi, ALU.subtract).then_inc(or_lo_ready, 1)
                elif kind == "B":
                    for f in range(KT):
                        if f < KT - 1:
                            dve.wait_ge(b_done, 7 * g + f + 1)
                        else:
                            dve.wait_ge(piece_used, n + 2)
                        dst = racc[:, f * TG:f * TG + TGn]
                        if x == 0:
                            ins = nc.vector.tensor_copy(dst, bank([2, 0, 1][f % 3], n=TGn))
                        else:
                            ins = tt(dst, dst, bank([2, 0, 1][f % 3], n=TGn), ALU.add)
                        ins.then_inc(racc_done, 1)
                elif kind == "MB":
                    dve.wait_ge(racc_done, 8 * HR * (G + 1))
                    for f in range(KT):
                        dve.wait_ge(sig_done, 16 * G + f + 1)
                        rf = racc[:, f * TG:f * TG + TGn]
                        tt(rf, rf, sig[:, f * TG:f * TG + TGn], ALU.mult).then_inc(mb_done, 1)
                elif kind == "KVA":
                    dve.wait_ge(piece_used, n + 2)
                    for t in range(3):
                        R = rows_of(3 * G + t)
                        a3, b3 = rope(G, R, bank(3 + t, R, 0, P), t, cs_att, HD // 2, HKV, None, None)
                        av = a3.rearrange("p (q s) c -> p q s c", s=2)
                        bv = b3.rearrange("p (q s) c -> p q s c", s=2)
                        ov = ka[0:R, t * P:(t + 1) * P].rearrange("p (q s c) -> p q s c", s=2, c=HD // 2)
                        tt(ov[:, :, 0, :], av[:, :, 0, :], bv[:, :, 1, :], ALU.subtract)
                        ins = tt(ov[:, :, 1, :], av[:, :, 1, :], bv[:, :, 0, :], ALU.add)
                        if t < 2:
                            link(ins)
                    ins.then_inc(ka_ready, 1)
                    dve.wait_ge(ka_ready, G + 1)
                elif kind == "TRQ":
                    t = x
                    R = rows_of(3 * G + t)
                    if t == 2:
                        dve.wait_ge(trq_done, 3 * G + 1)
                    a3, b3 = rope(G, R, bank(t, R), t, cs_att, HD // 2, HQ, None, None)
                    ob = qa[0:R, (t % 2) * 512:(t % 2 + 1) * 512].rearrange("p (g n s c) -> p n g s c", g=GQ, n=HKV, s=2)
                    av = a3.rearrange("p (n g s) c -> p n g s c", n=HKV, s=2)
                    bv = b3.rearrange("p (n g s) c -> p n g s c", n=HKV, s=2)
                    tt(ob[:, :, :, 0, :], av[:, :, :, 0, :], bv[:, :, :, 1, :], ALU.subtract)
                    tt(ob[:, :, :, 1, :], av[:, :, :, 1, :], bv[:, :, :, 0, :], ALU.add).then_inc(qa_ready, 1)
                    dve.wait_ge(qa_ready, 3 * G + t + 1)
                elif kind in ("AS", "SS"):
                    u = n_unit[0]
                    n_unit[0] += 1
                    wd = 2 * WIN if kind == "AS" else 192
                    pb = prob[:, (u % 2) * 1024:(u % 2) * 1024 + 4 * wd]
                    p3 = pb.rearrange("p (q c) -> p q c", q=4)
                    dve.wait_ge(as_done, u + 1)
                    if u >= 2:
                        dve.wait_ge(ap_done, u - 1)
                    if kind == "AS":
                        t, nkv = units_of(G)[x]
                        msk = att_mask[:, 256:512] if (G or t) else att_mask[:, 0:256]
                        ins = nc.vector.scalar_tensor_tensor(
                            out=p3, in0=ps[:, 3 * BANK:5 * BANK].rearrange("p (q c) -> p q c", q=4), scalar=HD ** -0.5,
                            in1=msk.unsqueeze(1).to_broadcast([P, 4, 256]), op0=ALU.mult, op1=ALU.add)
                        snk = sinks[:, nkv * 4:nkv * 4 + 4]
                    else:
                        for nkv in range(HKV):
                            ins = nc.vector.scalar_tensor_tensor(
                                out=pb[:, nkv * 384:(nkv + 1) * 384], in0=bank(3 + nkv, n=384), scalar=HD ** -0.5,
                                in1=att_mask_s[:], op0=ALU.mult, op1=ALU.add)
                    ins.then_inc(sm_read, 1)
                    dve.wait_ge(sm_read, u + 1)
                    link(nc.vector.tensor_reduce(mx[:, 0:4], p3, AXX, ALU.max))
                    if kind == "AS":
                        link(tt(mx[:, 0:4], mx[:, 0:4], snk, ALU.max))
                        tt(esd[:, 0:4], snk, mx[:, 0:4], ALU.subtract)
                    else:
                        s2 = sinks_s[:, :].unsqueeze(2).to_broadcast([P, 2, 2])
                        m2 = mx[:, 0:4].rearrange("p (n b) -> p n b", b=2)
                        link(tt(m2, m2, s2, ALU.max))
                        tt(esd[:, 0:4].rearrange("p (n b) -> p n b", b=2), s2, m2, ALU.subtract)
                    nc.vector.tensor_scalar(nmx[:, 0:4], mx[:, 0:4], -1.0, None, ALU.mult).then_inc(nmx_ready, 1)
                    dve.wait_ge(exp_done, u + 1)
                    link(tt(den[:, 0:4], rsum[:, 0:4], es[:, 0:4], ALU.add))
                    link(nc.vector.reciprocal(rden[:, 0:4], den[:, 0:4]))
                    tt(p3, p3, rden[:, 0:4].unsqueeze(2).to_broadcast([P, 4, wd]), ALU.mult).then_inc(p_ready, 1)
                elif (kind == "AV" and x % 2 == 1) or kind == "SV":
                    t = x // 2 if kind == "AV" else 2
                    R = rows_of(3 * G + t)
                    dve.wait_ge(oa_hi_ready, 3 * G + t + 1)
                    if kind == "SV":
                        for (par, nkv, src, hi), (_, _, _, lo) in zip(sample_heads(oaT_hi), sample_heads(oaT_lo)):
                            ins = tt(lo, src, fr(hi), ALU.subtract)
                        ins.then_inc(oa_lo_ready, 1)
                        continue
                    hi = fr(oaT_hi[:].rearrange("p (k c) -> p k c", k=4)[:, :, t * P:t * P + R])
                    lo = oaT_lo[:].rearrange("p (k c) -> p k c", k=4)[:, :, t * P:t * P + R]
                    tt(lo, bank(2).rearrange("p (k c) -> p k c", k=4)[:, :, 0:R], hi, ALU.subtract).then_inc(oa_lo_ready, 1)
                elif kind == "A":
                    dve.wait_ge(piece_used, n + 1)
                    dve.wait_ge(sig_done, 16 * (G + 1))
                    b0 = 0 if x % 2 == 0 else 3
                    for f2 in range(2):
                        sf = sig[:, (2 * x + f2) * TG:(2 * x + f2) * TG + TGn]
                        ins = tt(sf, sf, bank(b0 + f2, n=TGn), ALU.mult)
                    link(ins)
                    for f2 in range(2):
                        f = 2 * x + f2
                        sf = sig[:, f * TG:f * TG + TGn]
                        tt(sf, sf, racc[:, f * TG:f * TG + TGn], ALU.add).then_inc(m_ready, 1)
                    dve.wait_ge(m_hi_ready, 4 * G + x + 1)
                    src = sig[:, 2 * x * TG:(2 * x + 2) * TG].rearrange("p (f c) -> p f c", f=2)[:, :, 0:TGn]
                    b = (x % 2) * 2 * TG
                    hi = fr(mT_hi[:, b:b + 2 * TG].rearrange("p (f c) -> p f c", f=2)[:, :, 0:TGn])
                    lo = mT_lo[:, b:b + 2 * TG].rearrange("p (f c) -> p f c", f=2)[:, :, 0:TGn]
                    tt(lo, src, hi, ALU.subtract).then_inc(m_lo_ready, 1)
                elif kind == "WO":
                    for q in range(6):
                        t = 3 * G + q // 2
                        R = rows_of(t)
                        if x == 0 and q % 2 == 0:
                            dve.wait_ge(y_scaled, NT + t + 1)
                        if q < 5:
                            dve.wait_ge(wo_done, 5 * (4 * G + x) + q + 1)
                        else:
                            dve.wait_ge(piece_used, n + 2)
                        ysl = y[0:R, t * D + (q % 2) * 512:t * D + (q % 2) * 512 + 512]
                        tt(ysl, ysl, bank([2, 5, 6, 7][q % 4], R), ALU.add).then_inc(wacc_done, 1)
                elif kind == "LNS":
                    dve.wait_ge(wacc_done, 24 * (G + 1))
                    ln_stats(3 * G + x)
                elif kind == "LNH":
                    if 3 * G + x in DVE_AFFINE[1]:
                        affine(1, 3 * G + x)

            for t in range(6, NT):
                xT_evac(2 * NT + t, t, xT_hi, xT_lo, T, t * P)
            ffn(1, FFN2_0)
            for t in DVE_AFFINE[2]:
                affine(2, t)

        @block.tensor
        def _(pe):
            mm = nc.tensor.matmul

            def three(out, a_hi, a_lo, b_hi, b_lo, first, last):
                mm(out, a_hi, b_hi, start=first, stop=False)
                mm(out, a_hi, b_lo, start=False, stop=False)
                return mm(out, a_lo, b_hi, start=False, stop=last)

            def xT_pe(v, t):
                R = rows_of(t)
                same = [u for u in range(v) if xt_base(u) == xt_base(v)]
                if same:
                    pe.wait_ge(xT_lo_ready, same[-1] + 1)
                base = xt_base(v) * BANK
                for k in range(KT):
                    ins = nc.tensor.transpose(ps[:, base + k * P:base + k * P + R], y[0:R, t * D + k * P:t * D + (k + 1) * P],
                                              ident[0:R, 0:R])
                ins.then_inc(xt_done, 1)

            def up(b0, n):
                wh, wl = wslot(n, False), wslot(n, True)
                for k in range(KT):
                    for ci, (c0, cw) in enumerate(CHUNKS):
                        out = bank(b0 + ci, n=cw)
                        xh, xl = xT_hi[:, k * T + c0:k * T + c0 + cw], xT_lo[:, k * T + c0:k * T + c0 + cw]
                        mm(out, wh[:, k * P:(k + 1) * P], xh, start=(k == 0), stop=False)
                        mm(out, wh[:, k * P:(k + 1) * P], xl, start=False, stop=False)
                    for ci, (c0, cw) in enumerate(CHUNKS):
                        ins = mm(bank(b0 + ci, n=cw), wl[:, k * P:(k + 1) * P], xT_hi[:, k * T + c0:k * T + c0 + cw],
                                 start=False, stop=(k == KT - 1))
                ins.then_inc(piece_used, 1)

            def ffn(f, base):
                J0, I0 = NJ * f, NI * f

                def turn(i, peeled):
                    st_ = 0 if peeled else 6
                    n = base + 1 + (6 * i if peeled else 0)
                    J = i * 2 + J0
                    lastt = peeled and i == NI - 1
                    pe.wait_ge(lo_ready, n + 1 + st_ * i)
                    up(3, n)
                    pe.wait_ge(lo_ready, n + 2 + st_ * i)
                    pe.wait_ge(silu_done, J * 3 + 3)
                    up(0, n + 1)
                    pe.wait_ge(lo_ready, n + 3 + st_ * i)
                    pe.wait_ge(h_mul, J * 3 + 3)
                    up(3, n + 2)
                    if not lastt:
                        pe.wait_ge(lo_ready, n + 4 + st_ * i)
                        pe.wait_ge(silu_done, J * 3 + 6)
                        up(0, n + 3)
                    nw = n + (3 if lastt else 4)
                    pe.wait_ge(lo_ready, nw + 2 + st_ * i)
                    pe.wait_ge(h_lo_ready, J * 3 + 6)
                    if not (peeled and i == 0 and f == 0):
                        pe.wait_ge(acc_done, (i + I0) * 18)
                    for q in range(2 * NT):
                        t, half = q // 2, q % 2
                        R = rows_of(t)
                        if q >= 5:
                            pe.wait_ge(acc_done, (i + I0) * 18 + q - 4)
                        out = bank(DOWN_BANKS[q % 5], R)
                        for s in range(2):
                            a = s * T + t * P
                            ins = three(out, h_hi[:, a:a + R], h_lo[:, a:a + R],
                                        wslot(nw + s, False)[:, half * 512:(half + 1) * 512],
                                        wslot(nw + s, True)[:, half * 512:(half + 1) * 512], s == 0, s == 1)
                        ins.then_inc(*((down_done, 1) if q < 2 * NT - 1 else (piece_used, 2)))
                        if lastt and f == 0 and half and t >= 6:
                            wait_affine(pe, 0, t - 6)
                            xT_pe(NT + t - 6, t - 6)
                    pe.wait_ge(acc_done, (i + I0) * 18 + 16)

                wh, wl = wslot(base, False), wslot(base, True)
                for ci, (c0, cw) in enumerate(CHUNKS):
                    for t in range(3 * ci, 3 * ci + 3):
                        if f == 0:
                            pe.wait_ge(x_loaded[t], 16)
                            xT_pe(t, t)
                        elif t >= 6:
                            wait_affine(pe, 1, t)
                            xT_pe(2 * NT + t, t)
                    pe.wait_ge(xT_lo_ready, 2 * NT * f + max(3 * ci + 3, 6 * f))
                    pe.wait_ge(lo_ready, base + 1)
                    for k in range(KT):
                        xs = slice(k * T + c0, k * T + c0 + cw)
                        ins = three(bank(ci, n=cw), wh[:, k * P:(k + 1) * P], wl[:, k * P:(k + 1) * P],
                                    xT_hi[:, xs], xT_lo[:, xs], k == 0, k == KT - 1)
                ins.then_inc(piece_used, 1)
                turn(0, True)
                with pe.Fori(1, NI - 1) as i:
                    turn(i, False)
                turn(NI - 1, True)

            pe.wait_ge(ident_loaded, 16)
            ffn(0, 0)
            pe.wait_ge(acc_done, 18 * NI)

            def token_major(n, npieces, kper, width, b0, G):
                for i in range(npieces):
                    pe.wait_ge(lo_ready, n + i + 1)
                    wh, wl = wslot(n + i, False), wslot(n + i, True)
                    for kk in range(kper):
                        k = i * kper + kk
                        for t in range(3):
                            R = rows_of(3 * G + t)
                            a = k * TG + t * P
                            ins = three(bank(b0 + t, R, 0, width), xg_hi[:, a:a + R], xg_lo[:, a:a + R],
                                        wh[:, kk * width:(kk + 1) * width], wl[:, kk * width:(kk + 1) * width],
                                        k == 0, k == KT - 1)
                    ins.then_inc(piece_used, 1)

            def gate(n, b, G):
                TGn = tokens_of(G)
                pe.wait_ge(lo_ready, n + 1)
                wh, wl = wslot(n, False), wslot(n, True)
                for k in range(KT):
                    ins = three(bank(b, n=TGn), wh[:, k * P:(k + 1) * P], wl[:, k * P:(k + 1) * P],
                                xg_hi[:, k * TG:k * TG + TGn], xg_lo[:, k * TG:k * TG + TGn], k == 0, k == KT - 1)
                ins.then_inc(piece_used, 1)

            for kind, G, x, n in TIMELINE:
                g = HR * G + x
                TGn = tokens_of(G)
                last_group = G == NG - 1
                if kind == "XT":
                    pe.wait_ge(m_ready, KT * (G - 1) + 2 * x + 4)
                    xT_pe(NT + 3 * G + x, 3 * G + x)
                elif kind == "XF":
                    if x == 0:
                        pe.wait_ge(m_lo_ready, 4 * NG)
                    wait_affine(pe, 1, x)
                    xT_pe(2 * NT + x, x)
                elif kind == "P":
                    if x == 0:
                        pe.wait_ge(xT_lo_ready, NT + 3 * G + 3)
                        if G:
                            pe.wait_ge(wacc_done, 24 * G)
                    if g:
                        pe.wait_ge(rope_read, g)
                        pe.wait_ge(v_ready, g)
                        if x >= 2:
                            pe.wait_ge(qkT_ready, 2 * g)
                            if x == 3:
                                pe.wait_ge(racc_done, 8 * (g - 2))
                    token_major(n, 4, 2, 512, 0, G)
                elif kind == "G":
                    if g:
                        pe.wait_ge(gs_ready, g)
                        pe.wait_ge(r_ready, g)
                        if x >= 2:
                            pe.wait_ge(or_lo_ready, g - 1)
                    token_major(n, 2, 4, DV, 3, G)
                elif kind == "TR":
                    pe.wait_ge(rope_read, g + 1)
                    pe.wait_ge(v_ready, g + 1)
                    for s in range(2):
                        for t in range(3):
                            R = rows_of(3 * G + t)
                            ins = nc.tensor.transpose(bank(s, P, t * P, R),
                                                      qk[0:R, t * 2 * DK + s * DK:t * 2 * DK + (s + 1) * DK], ident[0:R, 0:R])
                    ins.then_inc(tr_done, 1)
                elif kind == "SKV":
                    pe.wait_ge(qkT_ready, 2 * g + 2)
                    if g:
                        pe.wait_ge(o_ready, g)
                        if last_group and x:
                            pe.wait_ge(st_ready, 2 * x)
                    for t in range(3):
                        R = rows_of(3 * G + t)
                        ins = mm(bank(6, R, t * P, R), kT[:, t * P:t * P + R], qT[:, t * P:t * P + R], start=True, stop=True)
                    ins.then_inc(s_done, 1)
                    pe.wait_ge(kdec_ready, g + 1)
                    pe.wait_ge(v_ready, g + 1)
                    vb, kb = (g % 2) * 3 * DV, (g % 2) * 3 * DK
                    for t in range(2):
                        ins = mm(bank(7, P, t * DV, DV), kdec[:, kb + t * DK:kb + (t + 1) * DK], v_r[:, vb + t * DV:vb + (t + 1) * DV],
                                 start=True, stop=True)
                    ins.then_inc(kv_done, 1)
                    if not last_group:
                        pe.wait_ge(gs_ready, g + 1)
                        mm(bank(3, P, 0, DV), kdec[:, kb + 2 * DK:kb + 3 * DK], v_r[:, vb + 2 * DV:vb + 3 * DV],
                           start=True, stop=True).then_inc(kv_done, 1)
                elif kind == "PVQ":
                    pe.wait_ge(pt_ready, g + 1)
                    pe.wait_ge(r_ready, g + 1)
                    vb = (g % 2) * 3 * DV
                    slot = (x - G) % 5
                    for t in range(3):
                        R = rows_of(3 * G + t)
                        sample = last_group and t == 2
                        out = ps[0:R, 6 * BANK + t * DV:6 * BANK + (t + 1) * DV]
                        no_state = G == 0 and t == 0
                        ins = mm(out, pt_r[0:R, t * P:t * P + R], v_r[0:R, vb + t * DV:vb + (t + 1) * DV],
                                 start=True, stop=no_state)
                        if sample:
                            pe.wait_ge(qTm_ready, x + 1)
                            pe.wait_ge(st_loaded, 16 * (x + 1))
                            for b in range(DB):
                                ins = mm(out, qT_m[:, b * SR:(b + 1) * SR], st[:, b * DV:(b + 1) * DV], start=False, stop=(b == DB - 1))
                        elif not no_state:
                            state = rst[:, slot * DV:(slot + 1) * DV] if t == 0 else r12[:, (t - 1) * DV:t * DV]
                            ins = mm(out, qT[:, t * P:t * P + R], state, start=False, stop=True)
                    ins.then_inc(pvq_done, 1)
                elif kind in ("SUa", "SUb"):
                    vb = (g % 2) * 3 * DV
                    for half in ([0] if kind == "SUa" else [1]):
                        if half == 0:
                            pe.wait_ge(o_ready, g + 1)
                        else:
                            pe.wait_ge(st_ready, 2 * x + 1)
                        pe.wait_ge(kdm_ready, 2 * x + half + 1)
                        for b in range(4):
                            ins = mm(ps[:, 6 * BANK + b * DV:6 * BANK + (b + 1) * DV], kdec_m[0:SR, b * DK:(b + 1) * DK],
                                     v_r[0:SR, vb + 2 * DV:vb + 3 * DV], start=True, stop=True)
                        ins.then_inc(su_done, 1)
                elif kind == "T":
                    pe.wait_ge(gn_done, g + 1)
                    if x < HR - 1:
                        pe.wait_ge(gs_ready, g + 2)
                    elif last_group:
                        pe.wait_ge(st_ready, 2 * HR)
                    for e in range(2):
                        for t in range(3):
                            R = rows_of(3 * G + t)
                            ins = nc.tensor.transpose(bank((4 if x < HR - 1 else 6) + e, P, t * P, R), orow[0:R, t * DV + e * P:t * DV + (e + 1) * P],
                                                      ident[0:R, 0:R])
                    ins.then_inc(t_done, 1)
                elif kind == "B":
                    pe.wait_ge(lo_ready, n + 2)
                    pe.wait_ge(or_lo_ready, g + 1)
                    pe.wait_ge(qkT_ready, 2 * min(HR * (G + 1), g + 3))
                    for f in range(KT):
                        if g or f >= 3:
                            pe.wait_ge(racc_done, 8 * g + max(f - 2, 0))
                        for e in range(2):
                            fs = slice(f * P, (f + 1) * P)
                            ins = three(bank([2, 0, 1][f % 3], n=TGn), wslot(n + e, False)[:, fs], wslot(n + e, True)[:, fs],
                                        orT_hi[:, e * TG:e * TG + TGn], orT_lo[:, e * TG:e * TG + TGn], e == 0, e == 1)
                        if f < KT - 1:
                            ins.then_inc(b_done, 1)
                    ins.then_inc(piece_used, 2)
                elif kind == "GB":
                    if x == 0:
                        pe.wait_ge(or_lo_ready, HR * G + 3)
                        pe.wait_ge(gs_ready, HR * (G + 1))
                    if x == 2:
                        pe.wait_ge(r_ready, HR * (G + 1))
                    if x >= 3:
                        pe.wait_ge(sig_done, 16 * G + x - 2)
                    gate(n, 3 + (x + 1) % 3, G)
                elif kind == "GA":
                    if x == 0:
                        pe.wait_ge(or_lo_ready, HR * (G + 1))
                        if last_group:
                            pe.wait_ge(kcT_ready, 1)
                    if x >= 2:
                        pe.wait_ge(sig_done, 16 * G + 8 + x - 1)
                    gate(n, 6 + x % 2, G)
                elif kind == "QA":
                    pe.wait_ge(racc_done, 8 * HR * (G + 1))
                    token_major(n, 4, 2, 512, 0, G)
                elif kind == "KVA":
                    pe.wait_ge(sig_done, 16 * G + 8)
                    token_major(n, 2, 4, 256, 3, G)
                elif kind == "TRK":
                    pe.wait_ge(ka_ready, G + 1)
                    pe.wait_ge(va_ready, G + 1)
                    for t in range(3):
                        R = rows_of(3 * G + t)
                        ins = nc.tensor.transpose(bank(5, P, t * P, R), ka[0:R, t * P:(t + 1) * P], ident[0:R, 0:R])
                    ins.then_inc(trk_done, 1)
                elif kind == "TRQ":
                    R = rows_of(3 * G + x)
                    pe.wait_ge(qa_ready, 3 * G + x + 1)
                    if x == 2:
                        pe.wait_ge(kaT_ready, G + 1)
                    for q in range(GQ):
                        ins = nc.tensor.transpose(bank(3 + x, P, q * P, R), qa[0:R, (x % 2) * 512 + q * P:(x % 2) * 512 + (q + 1) * P],
                                                  ident[0:R, 0:R])
                    ins.then_inc(trq_done, 1)
                elif kind == "KC":
                    pe.wait_ge(kc_loaded, 16)
                    pe.wait_ge(or_lo_ready, HR * NG)
                    for b in range(DB):
                        ins = nc.tensor.transpose(ps[:, 6 * BANK + b * P:6 * BANK + (b + 1) * P], prob[:, b * P:(b + 1) * P], ident[:])
                    ins.then_inc(kc_tr, 1)
                elif kind == "AS":
                    t, nkv = units_of(G)[x]
                    u = len(units_of(0)) * G + x
                    pe.wait_ge(kaT_ready, G + 1)
                    pe.wait_ge(qaT_ready, 3 * G + 3)
                    if u:
                        pe.wait_ge(sm_read, u)
                    pr = slice(nkv * HD, (nkv + 1) * HD)
                    for q in range(GQ):
                        ins = mm(ps[:, 3 * BANK + q * 256:3 * BANK + (q + 1) * 256],
                                 qaT[pr, t * 512 + q * P:t * 512 + (q + 1) * P], kaT[pr, t * P:(t + 2) * P], start=True, stop=True)
                    ins.then_inc(as_done, 1)
                elif kind == "AP":
                    u = len(units_of(0)) * G + x
                    pe.wait_ge(p_ready, u + 1)
                    if u:
                        pe.wait_ge(pT_ready, u)
                    pb = (u % 2) * 1024
                    for q in range(8):
                        ins = nc.tensor.transpose(ps[:, q * P:(q + 1) * P], prob[:, pb + q * P:pb + (q + 1) * P], ident[:])
                    ins.then_inc(ap_done, 1)
                elif kind == "AV":
                    t, nkv = units_of(G)[x]
                    u = len(units_of(0)) * G + x
                    pe.wait_ge(pT_ready, u + 1)
                    if nkv == 0 and 3 * G + t:
                        pe.wait_ge(oa_lo_ready, 3 * G + t)
                    for q in range(GQ):
                        r0 = (q % 2) * HD
                        out = ps[r0:r0 + HD, 2 * BANK + (2 * nkv + q // 2) * P:2 * BANK + (2 * nkv + q // 2 + 1) * P]
                        for s in range(2):
                            ins = mm(out, va[:, (t + s) * P + nkv * HD:(t + s) * P + (nkv + 1) * HD],
                                     probT[:, (2 * q + s) * P:(2 * q + s + 1) * P], start=(s == 0), stop=(s == 1))
                    ins.then_inc(av_done, 1)
                elif kind == "SS":
                    u = len(units_of(0)) * G + 4
                    pe.wait_ge(kcT_ready, 1)
                    pe.wait_ge(sm_read, u)
                    for bh in range(2):
                        for nkv in range(HKV):
                            pr = slice(nkv * HD, (nkv + 1) * HD)
                            for b4 in range(4):
                                b = bh * 4 + b4
                                lhs = qaT[pr, 2 * 512 + b * GQ * DT:2 * 512 + (b + 1) * GQ * DT]
                                o0 = (3 + nkv) * BANK + bh * 192
                                mm(ps[32 * b4:32 * b4 + 32, o0:o0 + P], lhs, kcT[pr, b * P:(b + 1) * P], start=True, stop=True)
                                ins = mm(ps[32 * b4:32 * b4 + 32, o0 + P:o0 + P + SR], lhs, kaT[pr, 3 * P:3 * P + SR],
                                         start=True, stop=True)
                    ins.then_inc(as_done, 1)
                elif kind == "SP":
                    u = len(units_of(0)) * G + 4
                    pe.wait_ge(p_ready, u + 1)
                    pe.wait_ge(pT_ready, u)
                    pb = (u % 2) * 1024
                    for q in range(4):
                        nc.tensor.transpose(bank(0, P, q * P, P), prob[:, pb + q * 192:pb + q * 192 + P], ident[:])
                    for q in range(4):
                        ins = nc.tensor.transpose(bank(1, SR, q * P, P), prob[:, pb + q * 192 + P:pb + (q + 1) * 192], ident[:])
                    ins.then_inc(ap_done, 1)
                elif kind == "SV":
                    u = len(units_of(0)) * G + 4
                    pe.wait_ge(pT_ready, u + 1)
                    pe.wait_ge(oa_lo_ready, 3 * G + 2)
                    pe.wait_ge(vc_loaded, 16)
                    for par in range(2):
                        for q in range(4):
                            nkv, bh = q // 2, q % 2
                            c0 = 2 * BANK + q * P
                            rows = slice(par * HD, (par + 1) * HD)
                            mm(ps[rows, c0:c0 + P], va[0:SR, 3 * P + nkv * HD:3 * P + (nkv + 1) * HD],
                               probT[0:SR, 512 + q * P:512 + (q + 1) * P], start=True, stop=False)
                            for b4 in range(4):
                                b = bh * 4 + b4
                                ins = mm(ps[rows, c0 + b4 * 32:c0 + (b4 + 1) * 32],
                                         vc[:, b * P + nkv * HD:b * P + (nkv + 1) * HD],
                                         probT[:, q * P + b4 * 32:q * P + (b4 + 1) * 32], start=False, stop=(b4 == 3))
                    ins.then_inc(av_done, 1)
                elif kind == "A":
                    pe.wait_ge(lo_ready, n + 1)
                    if x == 0:
                        pe.wait_ge(oa_lo_ready, 3 * G + 3)
                        pe.wait_ge(pT_ready, 6 * G + (6 if not last_group else 5))
                    if x == 2:
                        pe.wait_ge(m_ready, KT * G + 2)
                    if x == 3:
                        pe.wait_ge(m_ready, KT * G + 4)
                        if not last_group:
                            pe.wait_ge(xT_lo_ready, NT + 3 * G + 4)
                    b0 = 0 if x % 2 == 0 else 3
                    for f2 in range(2):
                        for k in range(4):
                            cs = slice(k * 256 + f2 * P, k * 256 + (f2 + 1) * P)
                            ins = three(bank(b0 + f2, n=TGn), wslot(n, False)[:, cs], wslot(n, True)[:, cs],
                                        oaT_hi[:, k * TG:k * TG + TGn], oaT_lo[:, k * TG:k * TG + TGn], k == 0, k == 3)
                    ins.then_inc(piece_used, 1)
                elif kind == "WO":
                    pe.wait_ge(lo_ready, n + 2)
                    pe.wait_ge(m_lo_ready, 4 * G + x + 1)
                    if x == 0:
                        pe.wait_ge(sig_done, 16 * (G + 1))
                    mb = (x % 2) * 2 * TG
                    for q in range(6):
                        t, half = q // 2, q % 2
                        R = rows_of(3 * G + t)
                        k = 24 * G + 6 * x + q
                        if q >= 4 or x:
                            pe.wait_ge(wacc_done, k - 3 if q >= 4 else 24 * G + 6 * x)
                        for f2 in range(2):
                            a = mb + f2 * TG + t * P
                            ins = three(bank([2, 5, 6, 7][q % 4], R), mT_hi[:, a:a + R], mT_lo[:, a:a + R],
                                        wslot(n + f2, False)[:, half * 512:(half + 1) * 512],
                                        wslot(n + f2, True)[:, half * 512:(half + 1) * 512], f2 == 0, f2 == 1)
                        if q < 5:
                            ins.then_inc(wo_done, 1)
                    ins.then_inc(piece_used, 2)

            ffn(1, FFN2_0)


DVE_AFFINE = {0: (), 1: (6, 7, 8), 2: (5, 6, 7, 8)}


def affine_count(k, t):
    mine = t in DVE_AFFINE[k]
    n = sum((u in DVE_AFFINE[q]) == mine for q in range(k + 1) for u in range(NT) if (q, u) <= (k, t))
    return mine, n


def kv_count(G, x):
    return 2 * (HR * G + x + 1) if G < NG - 1 else 2 * HR * (NG - 1) + x + 1


def shape_constants():
    f4 = np.float32
    c = {"ident": np.eye(P, dtype=f4)}
    e_att = (np.arange(0, HD, 2) / HD).astype(f4).astype(np.float64)
    e_ret = (np.arange(DK // 2, dtype=f4) * f4(1.0 / (DK // 2 - 1))).astype(np.float64)
    inv_att = f4(1.0) / (10000.0 ** e_att).astype(f4)
    inv_ret = f4(1.0) / (10000.0 ** e_ret).astype(f4)
    pos = np.zeros((NT, P), dtype=f4)
    pos[:NT - 1] = np.arange(SEQ, dtype=f4).reshape(NT - 1, P)
    pos[NT - 1, :SR] = PAST + np.arange(SR) % DT
    for name, inv in (("cs_att", inv_att), ("cs_ret", inv_ret)):
        ang = (pos[:, :, None] * inv[None, None, :]).astype(f4).astype(np.float64)
        cs = np.stack([np.cos(ang), np.sin(ang)], axis=2).astype(f4)
        c[name] = np.ascontiguousarray(cs.reshape(NG, 3, P, -1).transpose(2, 0, 1, 3).reshape(P, NG, -1))
    i = np.arange(P)
    scale = DK ** -0.5
    c["ret_mask"] = np.stack([(i[:, None] <= i[None, :]) * np.exp(-(i[:, None] + 1) * g) * scale for g in LOG_G], 1)\
        .reshape(P, HR * P).astype(f4)
    r = np.arange(SR)
    b, t = r // DT, r % DT
    same = (b[:, None] == b[None, :]) & (t[:, None] <= t[None, :])
    c["ret_mask_s"] = np.stack([same * np.exp(-(t[:, None] + 1) * g) * scale for g in LOG_G], 1).reshape(SR, HR * SR).astype(f4)
    kd, qd = np.zeros((P, 2 * HR)), np.zeros((P, 2 * HR))
    for h, g in enumerate(LOG_G):
        kd[:, h], qd[:, h] = np.exp((P - 1 - i) * g) * scale, np.exp((i + 1) * g)
        kd[:, HR + h], qd[:, HR + h] = np.exp((DT - 1 - i % DT) * g) * scale, np.exp((i % DT + 1) * g)
    c["kdec_t"], c["qdec_t"] = kd.astype(f4), qd.astype(f4)
    own = np.where(i[None, :] <= i[:, None], 0.0, NEG)
    prev = np.where(i[None, :] > i[:, None], 0.0, NEG)
    none = np.full((P, P), NEG)
    c["att_mask"] = np.concatenate([none, own, prev, own], 1).astype(f4)
    row_b, row_t = i // 32, i % DT
    ms = np.full((P, 2, 192), NEG)
    for bh in range(2):
        ms[:, bh, :P] = np.where(i[None, :] > row_t[:, None], 0.0, NEG)
        ms[:, bh, P:] = np.where((b[None, :] == (bh * 4 + row_b)[:, None]) & (t[None, :] <= row_t[:, None]), 0.0, NEG)
    c["att_mask_s"] = ms.reshape(P, 384).astype(f4)
    onehot = (b[None, :] == np.arange(DB)[:, None]).astype(f4)
    c["batch_cols"] = np.ascontiguousarray(np.broadcast_to(onehot.reshape(1, -1), (P, DB * SR)))
    c["batch_rows"] = np.ascontiguousarray(onehot.T)
    return c


_INS = ["x_prompt", "x_sample", "cache_k", "cache_v", "state_ret", "ln_g", "ln_b", "ffn_wi", "ffn_wo", "w_in",
        "w_br_attn", "w_br_ret", "w_o"]
_OUTS = [("y_prompt", (1, SEQ, D)), ("y_sample", (DB, DT, D)), ("kcp", (1, 1, WIN, HKV, HD)), ("vcp", (1, 1, WIN, HKV, HD)),
         ("rp", (1, 1, HR, DK, DV)), ("kcs", (1, DB, WIN, HKV, HD)), ("vcs", (1, DB, WIN, HKV, HD)),
         ("rs", (1, DB, HR, DK, DV))]


def kernel(**inputs):
    import concourse.bacc as _bacc
    from concourse.bass_utils import run_bass_kernel_spmd as _run

    nc = _bacc.Bacc("TRN2", target_bir_lowering=False, num_devices=1)
    arrays, w, c, o = {}, {}, {}, {}
    for name in _INS:
        a = np.ascontiguousarray(inputs[name])
        arrays[f"in_{name}"] = a
        w[name] = nc.dram_tensor(f"in_{name}", a.shape, F32, kind="ExternalInput").ap()
    for name in ("w_in", "w_br_attn", "w_br_ret", "w_o"):
        w[name] = w[name][0]
    consts = shape_constants()
    sk = np.asarray(inputs["attn_sinks"])[0]
    consts["sinks"] = np.ascontiguousarray(np.broadcast_to(sk[None, :], (P, HQ)))
    consts["sinks_s"] = np.ascontiguousarray(np.tile(np.repeat(sk.reshape(HKV, GQ).T, DT, axis=0), (4, 1)))
    for name, a in consts.items():
        arrays[f"c_{name}"] = a
        c[name] = nc.dram_tensor(f"c_{name}", a.shape, F32, kind="ExternalInput").ap()
    for name, shape in _OUTS:
        o[name] = nc.dram_tensor(f"out_{name}", shape, F32, kind="ExternalOutput").ap()
    hybrid_layer(nc, w, c, o)
    r = _run(nc, [arrays], core_ids=[0])
    return tuple(r.results[0][f"out_{name}"] for name, _ in _OUTS)
```
